# Optimizing a Trainium2 kernel written in Bass

```python
import jax
import jax.numpy as jnp
from jax import lax
import numpy as np

D_MODEL = 1024
BATCH = 1
SEQ = 256
DEPTH = 2

HEAD_DIM = 64
A_HEADS = 4
A_KV_HEADS = 2
A_GROUP = A_HEADS // A_KV_HEADS
A_WINDOW = 128
B_HEADS = 4
B_Q_RANK = 256
B_KV_RANK = 128
B_NOPE = 64
B_ROPE = 32
B_V = HEAD_DIM
ROPE_THETA = 10000.0
C_HEADS = 8
C_KV_HEADS = 2
C_GROUP = C_HEADS // C_KV_HEADS
C_CMP_BLOCK = 32
C_CMP_STRIDE = 16
C_CMP_HIDDEN = 128
C_SEL_BLOCK = 64
C_SEL_TOP = 16
C_WINDOW = 512
Q_BLOCK = 128
SEL_Q_BLOCK = 64
D_FF = 4096
N_EXPERTS = 8
TOP_K = 2
D_FF_EXPERT = 3584
NORM_EPS = 1e-6
NEG_INF = -1e30

A_Q_COLS = A_HEADS * HEAD_DIM
A_KV_COLS = A_KV_HEADS * HEAD_DIM
C_Q_COLS = C_HEADS * HEAD_DIM
C_KV_COLS = C_KV_HEADS * HEAD_DIM
C_GATE_COLS = C_HEADS * 3
IN_SPLITS = (A_Q_COLS, A_KV_COLS, A_KV_COLS, B_Q_RANK, B_KV_RANK, B_ROPE, C_Q_COLS,
             C_KV_COLS, C_KV_COLS, C_KV_COLS, C_KV_COLS, C_KV_COLS, C_KV_COLS, C_GATE_COLS)
N_IN = sum(IN_SPLITS)
MIX_WIDTH = A_HEADS * HEAD_DIM + B_HEADS * B_V + C_HEADS * HEAD_DIM

kernel_name = 'hybrid_swa_mla_nsa_moe_block'

def _rmsnorm(x, g):
    xf = x.astype(jnp.float32)
    y = xf * lax.rsqrt(jnp.mean(xf * xf, axis=-1, keepdims=True) + NORM_EPS)
    return (y * g.astype(jnp.float32)).astype(x.dtype)

def _alibi_slopes(n):
    return np.array([2.0 ** (-8.0 * (i + 1) / n) for i in range(n)], dtype=np.float32)

def _rope(x, pos):
    d = x.shape[-1]
    inv = (ROPE_THETA ** (-np.arange(0, d, 2, dtype=np.float32) / d)).astype(np.float32)
    ang = pos.astype(jnp.float32)[..., None] * inv
    cos = jnp.cos(ang)[:, :, None, :]
    sin = jnp.sin(ang)[:, :, None, :]
    xf = x.astype(jnp.float32)
    x1, x2 = xf[..., : d // 2], xf[..., d // 2:]
    return jnp.concatenate([x1 * cos - x2 * sin, x2 * cos + x1 * sin], axis=-1).astype(x.dtype)

def _banded_attention(q, k, v, window, slopes, sinks=None):
    B, S, G, R, dh = q.shape
    nb = S // Q_BLOCK
    span = Q_BLOCK + window
    kp = jnp.pad(k, ((0, 0), (window, 0), (0, 0), (0, 0)))
    vp = jnp.pad(v, ((0, 0), (window, 0), (0, 0), (0, 0)))
    idx = np.arange(nb)[:, None] * Q_BLOCK + np.arange(span)[None, :]
    kb = kp[:, idx]
    vb = vp[:, idx]
    qb = q.reshape(B, nb, Q_BLOCK, G, R, dh)
    s = jnp.einsum('bnqgrd,bnkgd->bngrqk', qb, kb).astype(jnp.float32) * (dh ** -0.5)
    dist = (np.arange(Q_BLOCK)[:, None] + window) - np.arange(span)[None, :]
    kabs = idx - window
    valid = (dist[None] >= 0) & (dist[None] < window) & (kabs[:, None, :] >= 0)
    s = s - slopes[None, None, :, :, None, None] * dist.astype(np.float32)
    s = jnp.where(valid[None, :, None, None], s, NEG_INF)
    if sinks is None:
        p = jax.nn.softmax(s, axis=-1)
    else:
        sk = sinks.astype(jnp.float32)[None, None, :, :, None, None]
        m = jnp.maximum(jnp.max(s, axis=-1, keepdims=True), sk)
        e = jnp.exp(s - m)
        p = e / (jnp.sum(e, axis=-1, keepdims=True) + jnp.exp(sk - m))
    o = jnp.einsum('bngrqk,bnkgd->bnqgrd', p.astype(v.dtype), vb)
    return o.reshape(B, S, G, R, dh)

def _causal_attention_blocks(q, k, v):
    B, S, H, dqk = q.shape
    dv = v.shape[-1]
    nb = S // Q_BLOCK
    scale = dqk ** -0.5
    qb = jnp.moveaxis(q.reshape(B, nb, Q_BLOCK, H, dqk), 1, 0)
    kpos = jnp.arange(S)

    def block(args):
        qi, start = args
        s = jnp.einsum('bqhd,bkhd->bhqk', qi, k).astype(jnp.float32) * scale
        qpos = start + jnp.arange(Q_BLOCK)
        s = jnp.where(kpos[None, :] <= qpos[:, None], s, NEG_INF)
        p = jax.nn.softmax(s, axis=-1).astype(v.dtype)
        return jnp.einsum('bhqk,bkhd->bqhd', p, v)

    o = lax.map(block, (qb, jnp.arange(nb) * Q_BLOCK))
    return jnp.moveaxis(o, 0, 1).reshape(B, S, H, dv)

def _nsa_attention(q, k_cmp, v_cmp, k_sel, v_sel, k_win, v_win, gates,
                   w1k, w2k, pek, w1v, w2v, pev, slopes):
    B, S, G, R, dh = q.shape
    scale = dh ** -0.5
    n_cmp = (S - C_CMP_BLOCK) // C_CMP_STRIDE + 1
    n_sel = S // C_SEL_BLOCK
    n_top = min(C_SEL_TOP, n_sel)
    t = np.arange(S)

    cstart = np.arange(n_cmp) * C_CMP_STRIDE
    cend = cstart + C_CMP_BLOCK - 1
    cidx = cstart[:, None] + np.arange(C_CMP_BLOCK)[None, :]

    def compress(xs, w1, w2, pe):
        blocks = xs[:, cidx] + pe[None, None, :, None, :]
        hid = jax.nn.gelu(jnp.einsum('bnlgd,lde->bnge', blocks, w1))
        return jnp.einsum('bnge,ed->bngd', hid, w2)

    kc = compress(k_cmp, w1k, w2k, pek)
    vc = compress(v_cmp, w1v, w2v, pev)
    cdist = (t[:, None] - cend[None, :]).astype(np.float32)
    cvalid = cdist >= 0
    s = jnp.einsum('bsgrd,bngd->bgrsn', q, kc).astype(jnp.float32) * scale
    s = s - slopes[None, :, :, None, None] * cdist
    s = jnp.where(cvalid, s, NEG_INF)
    has_cmp = (t >= C_CMP_BLOCK - 1).astype(np.float32)[:, None]
    p_cmp = jax.nn.softmax(s, axis=-1) * has_cmp
    o_cmp = jnp.einsum('bgrsn,bngd->bsgrd', p_cmp.astype(vc.dtype), vc)

    sstart = np.arange(n_sel) * C_SEL_BLOCK
    send = sstart + C_SEL_BLOCK - 1
    overlap = np.clip(np.minimum(cend[:, None], send[None, :]) - np.maximum(cstart[:, None], sstart[None, :]) + 1,
                      0, None).astype(np.float32) / C_CMP_STRIDE
    imp = jnp.einsum('bgrsn,nj->bgsj', p_cmp, overlap)
    cur = t // C_SEL_BLOCK
    jj = np.arange(n_sel)
    avail = sstart[None, :] <= t[:, None]
    forced = (jj[None, :] == 0) | (jj[None, :] == cur[:, None]) | (jj[None, :] == cur[:, None] - 1)
    imp = jnp.where(avail, imp, NEG_INF)
    imp = jnp.where(forced, -NEG_INF, imp)
    _, sel_idx = lax.top_k(imp, n_top)

    ksb = jnp.moveaxis(k_sel.reshape(B, n_sel, C_SEL_BLOCK, G, dh), 3, 1)
    vsb = jnp.moveaxis(v_sel.reshape(B, n_sel, C_SEL_BLOCK, G, dh), 3, 1)
    nc = S // SEL_Q_BLOCK
    q_ch = jnp.moveaxis(q.reshape(B, nc, SEL_Q_BLOCK, G, R, dh), 1, 0)
    i_ch = jnp.moveaxis(sel_idx.reshape(B, G, nc, SEL_Q_BLOCK, n_top), 2, 0)
    bi = jnp.arange(B)[:, None, None, None]
    gi = jnp.arange(G)[None, :, None, None]
    n_keys = n_top * C_SEL_BLOCK

    def sel_block(args):
        qi, ii, start = args
        kg = ksb[bi, gi, ii].reshape(B, G, SEL_Q_BLOCK, n_keys, dh)
        vg = vsb[bi, gi, ii].reshape(B, G, SEL_Q_BLOCK, n_keys, dh)
        tq = start + jnp.arange(SEL_Q_BLOCK)
        kpos = (ii[..., None] * C_SEL_BLOCK + jnp.arange(C_SEL_BLOCK)).reshape(B, G, SEL_Q_BLOCK, n_keys)
        dist = (tq[None, None, :, None] - kpos).astype(jnp.float32)[:, :, None]
        sc = jnp.einsum('bqgrd,bgqkd->bgrqk', qi, kg).astype(jnp.float32) * scale
        sc = sc - slopes[None, :, :, None, None] * dist
        sc = jnp.where(dist >= 0, sc, NEG_INF)
        p = jax.nn.softmax(sc, axis=-1).astype(vg.dtype)
        return jnp.einsum('bgrqk,bgqkd->bqgrd', p, vg)

    o_slc = lax.map(sel_block, (q_ch, i_ch, jnp.arange(nc) * SEL_Q_BLOCK))
    o_slc = jnp.moveaxis(o_slc, 0, 1).reshape(B, S, G, R, dh)

    o_win = _banded_attention(q, k_win, v_win, C_WINDOW, slopes)

    return gates[..., 0:1] * o_cmp + gates[..., 1:2] * o_slc + gates[..., 2:3] * o_win

def _hybrid_mixer(h, positions, w_in, a_sinks, g_cq, w_uq, g_ckv, w_ukv,
                  c_w1_k, c_w2_k, c_pe_k, c_w1_v, c_w2_v, c_pe_v, g_oa, g_ob, g_oc, w_o):
    B, S, _ = h.shape
    proj = jnp.einsum('bsd,dn->bsn', h, w_in)
    cuts = np.cumsum(IN_SPLITS)[:-1].tolist()
    (a_q, a_k, a_v, b_cq, b_ckv, b_kr, c_q,
     c_kc, c_vc, c_ks, c_vs, c_kw, c_vw, c_g) = jnp.split(proj, cuts, axis=-1)

    qa = a_q.reshape(B, S, A_KV_HEADS, A_GROUP, HEAD_DIM)
    ka = a_k.reshape(B, S, A_KV_HEADS, HEAD_DIM)
    va = a_v.reshape(B, S, A_KV_HEADS, HEAD_DIM)
    a_slopes = jnp.asarray(_alibi_slopes(A_HEADS).reshape(A_KV_HEADS, A_GROUP))
    o_a = _banded_attention(qa, ka, va, A_WINDOW, a_slopes,
                            a_sinks.reshape(A_KV_HEADS, A_GROUP)).reshape(B, S, A_HEADS * HEAD_DIM)

    q_b = jnp.einsum('bsr,rn->bsn', _rmsnorm(b_cq, g_cq), w_uq).reshape(B, S, B_HEADS, B_NOPE + B_ROPE)
    q_b = jnp.concatenate([q_b[..., :B_NOPE], _rope(q_b[..., B_NOPE:], positions)], axis=-1)
    kv_b = jnp.einsum('bsr,rn->bsn', _rmsnorm(b_ckv, g_ckv), w_ukv).reshape(B, S, B_HEADS, B_NOPE + B_V)
    k_rope = jnp.broadcast_to(_rope(b_kr[:, :, None, :], positions), (B, S, B_HEADS, B_ROPE))
    k_b = jnp.concatenate([kv_b[..., :B_NOPE], k_rope], axis=-1)
    o_b = _causal_attention_blocks(q_b, k_b, kv_b[..., B_NOPE:]).reshape(B, S, B_HEADS * B_V)

    kv_shape = (B, S, C_KV_HEADS, HEAD_DIM)
    gates = jax.nn.sigmoid(c_g.astype(jnp.float32)).astype(h.dtype).reshape(B, S, C_KV_HEADS, C_GROUP, 3)
    c_slopes = jnp.asarray(_alibi_slopes(C_HEADS).reshape(C_KV_HEADS, C_GROUP))
    o_c = _nsa_attention(c_q.reshape(B, S, C_KV_HEADS, C_GROUP, HEAD_DIM),
                         c_kc.reshape(kv_shape), c_vc.reshape(kv_shape),
                         c_ks.reshape(kv_shape), c_vs.reshape(kv_shape),
                         c_kw.reshape(kv_shape), c_vw.reshape(kv_shape), gates,
                         c_w1_k, c_w2_k, c_pe_k, c_w1_v, c_w2_v, c_pe_v, c_slopes).reshape(B, S, C_HEADS * HEAD_DIM)

    mixed = jnp.concatenate([_rmsnorm(o_a, g_oa), _rmsnorm(o_b, g_ob), _rmsnorm(o_c, g_oc)], axis=-1)
    return jnp.einsum('bsm,md->bsd', mixed, w_o)

def _swiglu(h, wg, wu, wd):
    a = jnp.einsum('bsd,df->bsf', h, wg)
    b = jnp.einsum('bsd,df->bsf', h, wu)
    return jnp.einsum('bsf,fd->bsd', jax.nn.silu(a) * b, wd)

def _moe(h, w_router, w_gate, w_up, w_down):
    logits = jnp.einsum('bsd,de->bse', h, w_router).astype(jnp.float32)
    top_v, top_i = lax.top_k(logits, TOP_K)
    top_w = jax.nn.softmax(top_v, axis=-1)
    combine = jnp.sum(jax.nn.one_hot(top_i, N_EXPERTS, dtype=jnp.float32) * top_w[..., None], axis=-2)
    combine = combine.astype(h.dtype)
    y = jnp.zeros_like(h)
    for e in range(N_EXPERTS):
        y = y + combine[..., e:e + 1] * _swiglu(h, w_gate[e], w_up[e], w_down[e])
    return y

def setup_inputs(seed: int = 0) -> dict:
    key = jax.random.key(seed)
    ks = jax.random.split(key, 32)
    n_dense = (DEPTH + 1) // 2
    n_moe = DEPTH // 2
    f32 = jnp.float32

    def nrm(k, shape, scale):
        return jax.random.normal(k, shape, f32) * scale

    def gain(k, shape):
        return 1.0 + 0.1 * jax.random.normal(k, shape, f32)

    x = jax.random.normal(ks[0], (BATCH, SEQ, D_MODEL), f32)
    offset = jax.random.randint(ks[1], (BATCH, 1), 0, 1024, dtype=jnp.int32)
    positions = (offset + jnp.arange(SEQ, dtype=jnp.int32)[None, :]).astype(jnp.int32)
    return {
        'x': x,
        'positions': positions,
        'w_in': nrm(ks[2], (DEPTH, D_MODEL, N_IN), D_MODEL ** -0.5),
        'a_sinks': nrm(ks[3], (DEPTH, A_HEADS), 0.5),
        'g_cq': gain(ks[4], (DEPTH, B_Q_RANK)),
        'w_uq': nrm(ks[5], (DEPTH, B_Q_RANK, B_HEADS * (B_NOPE + B_ROPE)), B_Q_RANK ** -0.5),
        'g_ckv': gain(ks[6], (DEPTH, B_KV_RANK)),
        'w_ukv': nrm(ks[7], (DEPTH, B_KV_RANK, B_HEADS * (B_NOPE + B_V)), B_KV_RANK ** -0.5),
        'c_w1_k': nrm(ks[8], (DEPTH, C_CMP_BLOCK, HEAD_DIM, C_CMP_HIDDEN), (C_CMP_BLOCK * HEAD_DIM) ** -0.5),
        'c_w2_k': nrm(ks[9], (DEPTH, C_CMP_HIDDEN, HEAD_DIM), C_CMP_HIDDEN ** -0.5),
        'c_pe_k': nrm(ks[10], (DEPTH, C_CMP_BLOCK, HEAD_DIM), 0.1),
        'c_w1_v': nrm(ks[11], (DEPTH, C_CMP_BLOCK, HEAD_DIM, C_CMP_HIDDEN), (C_CMP_BLOCK * HEAD_DIM) ** -0.5),
        'c_w2_v': nrm(ks[12], (DEPTH, C_CMP_HIDDEN, HEAD_DIM), C_CMP_HIDDEN ** -0.5),
        'c_pe_v': nrm(ks[13], (DEPTH, C_CMP_BLOCK, HEAD_DIM), 0.1),
        'g_oa': gain(ks[14], (DEPTH, A_HEADS * HEAD_DIM)),
        'g_ob': gain(ks[15], (DEPTH, B_HEADS * B_V)),
        'g_oc': gain(ks[16], (DEPTH, C_HEADS * HEAD_DIM)),
        'w_o': nrm(ks[17], (DEPTH, MIX_WIDTH, D_MODEL), MIX_WIDTH ** -0.5),
        'g_pre_mix': gain(ks[18], (DEPTH, D_MODEL)),
        'g_post_mix': gain(ks[19], (DEPTH, D_MODEL)),
        'g_pre_ffn': gain(ks[20], (DEPTH, D_MODEL)),
        'g_post_ffn': gain(ks[21], (DEPTH, D_MODEL)),
        'ffn_w_gate': nrm(ks[22], (n_dense, D_MODEL, D_FF), D_MODEL ** -0.5),
        'ffn_w_up': nrm(ks[23], (n_dense, D_MODEL, D_FF), D_MODEL ** -0.5),
        'ffn_w_down': nrm(ks[24], (n_dense, D_FF, D_MODEL), D_FF ** -0.5),
        'moe_router': nrm(ks[25], (n_moe, D_MODEL, N_EXPERTS), D_MODEL ** -0.5),
        'moe_w_gate': nrm(ks[26], (n_moe, N_EXPERTS, D_MODEL, D_FF_EXPERT), D_MODEL ** -0.5),
        'moe_w_up': nrm(ks[27], (n_moe, N_EXPERTS, D_MODEL, D_FF_EXPERT), D_MODEL ** -0.5),
        'moe_w_down': nrm(ks[28], (n_moe, N_EXPERTS, D_FF_EXPERT, D_MODEL), D_FF_EXPERT ** -0.5),
    }

def reference(x, positions, w_in, a_sinks, g_cq, w_uq, g_ckv, w_ukv, c_w1_k, c_w2_k, c_pe_k,
              c_w1_v, c_w2_v, c_pe_v, g_oa, g_ob, g_oc, w_o, g_pre_mix, g_post_mix, g_pre_ffn,
              g_post_ffn, ffn_w_gate, ffn_w_up, ffn_w_down, moe_router, moe_w_gate, moe_w_up,
              moe_w_down):
    for l in range(DEPTH):
        h = _rmsnorm(x, g_pre_mix[l])
        m = _hybrid_mixer(h, positions, w_in[l], a_sinks[l], g_cq[l], w_uq[l], g_ckv[l], w_ukv[l],
                          c_w1_k[l], c_w2_k[l], c_pe_k[l], c_w1_v[l], c_w2_v[l], c_pe_v[l],
                          g_oa[l], g_ob[l], g_oc[l], w_o[l])
        x = x + _rmsnorm(m, g_post_mix[l])
        h = _rmsnorm(x, g_pre_ffn[l])
        if l % 2 == 0:
            f = _swiglu(h, ffn_w_gate[l // 2], ffn_w_up[l // 2], ffn_w_down[l // 2])
        else:
            f = _moe(h, moe_router[l // 2], moe_w_gate[l // 2], moe_w_up[l // 2], moe_w_down[l // 2])
        x = x + _rmsnorm(f, g_post_ffn[l])
    return x


_drawn_inputs = setup_inputs


def setup_inputs(seed=0):
    import zlib

    import numpy as np

    out = dict(_drawn_inputs(seed))
    spreads = {}
    factors = {'c_pe_k': 2.933}
    for name, (base, spread) in spreads.items():
        noise = np.random.default_rng([zlib.crc32(name.encode()), seed]).standard_normal(out[name].shape)
        drawn = base * np.exp(spread * noise) if base else spread * noise
        out[name] = jnp.asarray(drawn.astype(out[name].dtype))
    for name, factor in factors.items():
        out[name] = (out[name] * factor).astype(out[name].dtype)
    return out
```

```python
from contextlib import ExitStack

import numpy as np

import concourse.bass as bass
from concourse import mybir

ALU = mybir.AluOpType
ACT = mybir.ActivationFunctionType
F32 = mybir.dt.float32
BF16 = mybir.dt.bfloat16
F32R = mybir.dt.float32r
I32 = mybir.dt.int32
AX_X = mybir.AxisListType.X

P = 128
D = 1024
S = 256
NT = S // P
DEPTH = 2
KD = D // P
EPS = 1e-6
HEAD = 64
A_HEADS, A_KV, A_WINDOW = 4, 2, 128
B_HEADS, B_QR, B_KVR, B_NOPE, B_ROPE = 4, 256, 128, 64, 32
C_HEADS, C_KV = 8, 2
CMP_BLOCK, CMP_STRIDE = 32, 16
N_CMP = (S - CMP_BLOCK) // CMP_STRIDE + 1
D_FF, D_FFE, N_EXP = 4096, 3584, 8
N_IN = 2232
QK_SCALE = HEAD ** -0.5
B_SCALE = (B_NOPE + B_ROPE) ** -0.5
MASKED = -1e30
TWO_PI = 2.0 * np.pi
PI_1 = 6.28125
PI_2 = float(np.float32(int((TWO_PI - PI_1) * 2 ** 20) / 2 ** 20))
PI_3 = float(TWO_PI - PI_1 - PI_2)
ROUND = 1.5 * 2 ** 23
SIN_MAX = 3.1415925
GELU_C = 2.0 * float(np.sqrt(2.0 / np.pi))

PIECE = 2048
RING = 6
SPLITS = 3
FCH = 512
ECH = D_FFE // FCH
DCH = D_FF // FCH
HALF_K = PIECE // FCH
HALF_F = PIECE // D
W_IN_CUTS = (0, 256, 512, 768, 928, 1184, 1440, 1696, 1952, 2208, N_IN)
N_W_IN = len(W_IN_CUTS) - 1
N_MIXER = N_W_IN + KD // HALF_F
MIXER_AT = (0, N_MIXER + 6 * DCH)
DENSE_AT = N_MIXER
MOE_AT = MIXER_AT[1] + N_MIXER

A_SLOPES = [2.0 ** (-8.0 * (i + 1) / A_HEADS) for i in range(A_HEADS)]
C_SLOPES = [2.0 ** (-8.0 * (i + 1) / C_HEADS) for i in range(C_HEADS)]
JOBS = [("A", h) for h in range(A_HEADS)] + [("B", h) for h in range(B_HEADS)] \
    + [("S", h) for h in range(C_HEADS)] + [("W", h) for h in range(C_HEADS)]
NJ = len(JOBS)
SPAN = 3 * P

CONSTS = [("ident", P), ("tri", P), ("iota", P), ("dist_a", SPAN), ("dist_c", SPAN), ("mask_b", SPAN),
          ("dist_cmp", NT * N_CMP), ("inv_freq", B_ROPE // 2), ("has_cmp", NT)]
COL = {}
_at = 0
for _n, _w in CONSTS:
    COL[_n] = (_at, _w)
    _at += _w
N_CONST = _at


def constants():
    q = np.arange(P)[:, None]
    far = MASKED * 3.0
    span = np.concatenate([q - np.arange(P)[None], q + P - np.arange(2 * P)[None]], axis=1).astype(np.float32)
    cend = np.arange(N_CMP) * CMP_STRIDE + CMP_BLOCK - 1
    tok = np.arange(S).reshape(NT, P).T
    cmp_d = (tok[:, :, None] - cend[None, None]).astype(np.float32)
    t = {
        "ident": np.eye(P), "tri": np.triu(np.ones((P, P))),
        "iota": np.broadcast_to(np.arange(P), (P, P)),
        "dist_a": np.where((span >= 0) & (span < A_WINDOW), -span, far),
        "dist_c": np.where(span >= 0, -span, far),
        "mask_b": np.where(span >= 0, 0.0, MASKED),
        "dist_cmp": np.where(cmp_d >= 0, -cmp_d, far).reshape(P, -1),
        "inv_freq": np.broadcast_to(10000.0 ** (-np.arange(0, B_ROPE, 2, dtype=np.float32) / B_ROPE), (P, B_ROPE // 2)),
        "has_cmp": (tok >= CMP_BLOCK - 1),
    }
    return np.ascontiguousarray(np.concatenate([np.asarray(t[n], np.float32) for n, _ in CONSTS], axis=1))


class Stage:

    def __init__(self, sem, per_round):
        self.sem, self.per_round = sem, per_round

    def at(self, rnd, k):
        return rnd * self.per_round + k


def decoder_kernel(nc, x_in, pos_in, consts_in, w, out):
    with ExitStack() as ctx:
        def sb(name, shape, dt=F32):
            return ctx.enter_context(nc.sbuf_tensor(name, shape, dt))

        def stage(name, per_round):
            return Stage(ctx.enter_context(nc.semaphore(name)), per_round)

        ps = ctx.enter_context(nc.psum_tensor("ps", [P, 8, 512], F32))

        def view(t, off, dims, p0=0, np_=P):
            pitch = 1
            for n in t.shape[1:]:
                pitch *= n
            return bass.AP(t, p0 * pitch + off, [[pitch, np_]] + [list(d) for d in dims])

        zone_at = -(-nc.sbuf_base // 32) * 32
        zone = sb("zone", [P, 16384])

        def split_view(name, off, dims):
            return nc.alloc_sbuf_tensor_at(name, [P] + dims, F32R, offset=zone_at + 4 * off)

        raw = sb("raw", [P, RING, PIECE])
        w_hi = sb("w_hi", [P, SPLITS, PIECE], F32R)
        w_lo = sb("w_lo", [P, SPLITS, PIECE], F32R)
        w1 = sb("w1", [P, 2, 16 * P])
        x = sb("x", [P, NT, D])
        con = sb("con", [P, N_CONST])
        ones = sb("ones", [P, P])
        zero16 = sb("zero16", [P, 512], BF16)
        w_uq = sb("w_uq", [P, 2, 384])
        w_ukv = sb("w_ukv", [P, 512])
        w2 = sb("w2", [P, 2, HEAD])
        pe_raw = sb("pe_raw", [16, 2, P])
        pe_t = sb("pe_t", [P, 2, 16])
        router = sb("router", [P, KD, N_EXP])
        g_post = sb("g_post", [P, D])
        g_pre = sb("g_pre", [P, 4, KD])
        g_out = sb("g_out", [P, DEPTH, KD])
        g_cq = sb("g_cq", [P, DEPTH, 2])
        g_ckv = sb("g_ckv", [P, DEPTH])
        sinks = sb("sinks", [P, DEPTH, A_HEADS])
        neg_sinks = sb("neg_sinks", [P, DEPTH, A_HEADS])
        pos_i = sb("pos_i", [P, NT], I32)
        pos_f = sb("pos_f", [P, NT])
        ang = sb("ang", [P, 2, NT, 16])
        turns = sb("turns", [P, 2, NT, 16])
        sincos = sb("sincos", [P, 2, NT, 16])
        v_cmp = sb("v_cmp", [P, C_KV, 256])
        kc_t = sb("kc_t", [P, 16])
        mean = sb("mean", [P, 8])
        rstd = sb("rstd", [P, 8])
        var = sb("var", [P, 8])
        minus_half = sb("minus_half", [P, 8])
        nmax = sb("nmax", [P, NJ, 2])
        rsum = sb("rsum", [P, NJ, 2])
        rinv = sb("rinv", [P, NJ, 2])
        sink_e = sb("sink_e", [P, A_HEADS, 2])
        gate = sb("gate", [P, NT, 3 * C_HEADS])
        gscale = sb("gscale", [P, NT, C_HEADS])
        cmax = sb("cmax", [P, 16])
        csum = sb("csum", [P, 16])
        rt = sb("rt", [P, 12, 16])
        cnt = sb("cnt", [P, 4])
        over = sb("over", [P, 1], I32)

        def c(name):
            a, n = COL[name]
            return con[:, a:a + n]

        def zv(off, *dims):
            n = 1
            for d in dims:
                n *= d
            v = zone[:, off:off + n]
            if len(dims) == 2:
                v = v.rearrange("p (a b) -> p a b", b=dims[1])
            if len(dims) == 3:
                v = v.rearrange("p (a b c) -> p a b c", b=dims[1], c=dims[2])
            return v

        HN, HT, FO = 0, 2048, 4096
        hn = zv(HN, NT, D)
        h_hi = split_view("h_hi", HT, [KD, S])
        h_lo = split_view("h_lo", FO, [KD, S])
        f_acc = zv(FO, NT, D)
        o_all = f_acc
        blk = zv(HN, 2, 480)
        c_tmp = zv(HN, 512)
        pt = zv(HN + 1024, 2, SPAN)
        sc_sb = zv(HT, 5, SPAN)
        pt_cmp = zv(HN + 512, 4, P)
        Z = 6144
        aq_t = zv(Z, 2, S)
        akv = zv(Z + 512, 512)
        cq_t = zv(Z + 1024, 4, S)
        mix_hi = split_view("mix_hi", Z, [KD, S])
        mix_lo = split_view("mix_lo", Z + 2048, [KD, S])
        KS, KW, XS, BL = Z + 2048, Z + 2560, Z + 3072, Z + 4096
        ksv = zv(KS, 512)
        kwv = zv(KW, 512)
        bl = zv(BL, NT, 416)
        CQN = BL + 832
        cqn_t = zv(CQN, 3, S)
        qn = zv(CQN + 768, NT, 256)
        kvb = zv(CQN + 1280, NT, 512)
        ROPE_IN = CQN + 2304
        ROPE_A, ROPE_B, ROPE_O = ROPE_IN + 320, ROPE_IN + 640, ROPE_IN + 960
        p_cmp = zv(ROPE_IN, 16, 32)
        hid = zv(ROPE_IN + 512, 4, 64)
        QN_T = ROPE_O + 512
        qn_t = zv(QN_T, 2, S)
        kn_t = zv(QN_T + 512, 2, S)
        qkr_t = zv(QN_T + 1024, 2, S)
        assert QN_T + 1536 <= 16384
        hg_hi = split_view("hg_hi", 6144, [KD, P])
        hg_lo = split_view("hg_lo", 7168, [KD, P])
        act_hi = split_view("act_hi", 8192, [NT, FCH])
        act_lo = split_view("act_lo", 9216, [NT, FCH])
        sil = zv(10240, NT, FCH)
        y_sb = zv(11264, 2, 512)
        sel = zv(12288, NT, P)
        sel_w = zv(12544, NT, P)
        sel_wt = zv(12800, NT, P)

        x_landed = stage("x_landed", 0)
        con_landed = stage("con_landed", 0)
        gpre_landed = stage("gpre_landed", 0)
        small_landed = stage("small_landed", 0)
        aux_landed = stage("aux_landed", 16 * 6)
        gpost_landed = stage("gpost_landed", 16)
        slot_landed = [stage(f"slot_landed{i}", 0) for i in range(RING)]
        w1_landed = stage("w1_landed", 32)
        hi_ready = stage("hi_ready", 0)
        lo_ready = stage("lo_ready", 0)
        piece_used = stage("piece_used", 0)
        out_stored = stage("out_stored", 0)
        setup_done = stage("setup_done", 0)
        sin_ready = stage("sin_ready", 0)
        sin_done = stage("sin_done", 0)
        pre_sq = stage("pre_sq", NT)
        pre_rstd = stage("pre_rstd", NT)
        post_rstd = stage("post_rstd", NT)
        lat_rstd = stage("lat_rstd", 1)
        o_rstd = stage("o_rstd", 1)
        pool_chain = stage("pool_chain", 0)
        hn_ready = stage("hn_ready", NT)
        hn_turned = stage("hn_turned", 4)
        h_gained = stage("h_gained", 4)
        hhi_ready = stage("hhi_ready", 4)
        h_ready = stage("h_ready", 4)
        post_sq = stage("post_sq", NT)
        x_updated = stage("x_updated", NT)
        proj_out_a = stage("proj_out_a", 7)
        proj_out_d = stage("proj_out_d", 6)
        lat_sq = stage("lat_sq", 4)
        lat_ready = stage("lat_ready", 1)
        lat_turned = stage("lat_turned", 2)
        latt_ready = stage("latt_ready", 2)
        latup_done = stage("latup_done", 4)
        latup_out = stage("latup_out", 4)
        kv_out = stage("kv_out", 2)
        qk_ready = stage("qk_ready", 1)
        qk_turned = stage("qk_turned", 3)
        qk_out = stage("qk_out", 3)
        pe_turned = stage("pe_turned", 1)
        blk_ready = stage("blk_ready", 2)
        hid_done = stage("hid_done", 2)
        gelu_arg = stage("gelu_arg", 1)
        gelu_exp = stage("gelu_exp", 1)
        gelu_ready = stage("gelu_ready", 1)
        ckv_done = stage("ckv_done", 2)
        ckv_out = stage("ckv_out", 1)
        cs_done = stage("cs_done", 1)
        cs_arg = stage("cs_arg", 1)
        cs_exp = stage("cs_exp", 1)
        cp_turned = stage("cp_turned", 1)
        cp_out = stage("cp_out", 1)
        co_done = stage("co_done", 1)
        co_out = stage("co_out", 1)
        score_done = stage("score_done", NJ)
        biased = stage("biased", NJ)
        max_ready = stage("max_ready", NJ)
        probs_ready = stage("probs_ready", NJ)
        probs_turned = stage("probs_turned", NJ)
        pt_ready_a = stage("pt_ready_a", NJ // 2)
        pt_ready_d = stage("pt_ready_d", NJ // 2)
        pv_done = stage("pv_done", NJ)
        sink_arg = stage("sink_arg", 1)
        sink_exp = stage("sink_exp", 1)
        o_out = stage("o_out", 4)
        o_sq = stage("o_sq", 6)
        mixed_ready = stage("mixed_ready", 1)
        mixed_turned = stage("mixed_turned", 4)
        mix_gained = stage("mix_gained", 4)
        mixhi_ready = stage("mixhi_ready", 4)
        mix_ready = stage("mix_ready", 4)
        silu_ready = stage("silu_ready", 0)
        prod_ready = stage("prod_ready", 0)
        act_turned = stage("act_turned", 0)
        acthi_ready = stage("acthi_ready", 0)
        act_ready = stage("act_ready", 0)
        logit_done = stage("logit_done", 0)
        route_arg = stage("route_arg", 0)
        route_exp = stage("route_exp", 0)
        picks_ready = stage("picks_ready", 0)
        ranks_done = stage("ranks_done", 0)
        over_ready = stage("over_ready", 0)
        f_zeroed = stage("f_zeroed", 0)
        slots_shifted = stage("slots_shifted", 0)
        f_summed = stage("f_summed", 0)
        sel_ready = stage("sel_ready", 0)
        gathered = stage("gathered", 0)
        hg_gained = stage("hg_gained", 0)
        hghi_ready = stage("hghi_ready", 0)
        hg_ready = stage("hg_ready", 0)
        selw_ready = stage("selw_ready", 0)
        selw_turned = stage("selw_turned", 0)
        selwt_ready = stage("selwt_ready", 0)
        y_ready = stage("y_ready", 0)
        scattered = stage("scattered", 0)
        added = stage("added", 0)
        dve_chain = stage("dve_chain", 0)

        def wait_piece(eng, stage_, n, r):
            eng.wait_ge(stage_.sem, r * RING + (n + 1))

        block = ctx.enter_context(nc.Block())

        @block.sync
        def _(sp):
            def load(n, r, src, k):
                if n >= RING or not isinstance(r, int):
                    wait_piece(sp, lo_ready, n - RING, r)
                width = src.shape[-1]
                sp.dma_start(raw[:, n % RING, 0:k * width].rearrange("p (k n) -> p k n", k=k), src
                             ).then_inc(slot_landed[n % RING].sem, 16)

            def w_in_piece(layer, i):
                a, b = W_IN_CUTS[i], W_IN_CUTS[i + 1]
                load(MIXER_AT[layer] + i, 0, w["w_in"][layer].rearrange("(p k) n -> p k n", k=KD)[:, :, a:b], KD)

            def w_o_piece(layer, i):
                load(MIXER_AT[layer] + N_W_IN + i, 0, w["w_o"][layer].rearrange("(p k) n -> p k n", k=KD)
                     [:, HALF_F * i:HALF_F * (i + 1), :], HALF_F)

            def up_pieces(n, r, wt, ch):
                for half in range(2):
                    load(n + half, r, wt.rearrange("(p k) (c n) -> c p k n", k=KD, n=FCH)[ch]
                         [:, HALF_K * half:HALF_K * (half + 1), :], HALF_K)

            def down_pieces(n, r, wt, ch):
                for half in range(2):
                    load(n + half, r, wt.rearrange("(c f p) n -> c p f n", p=P, f=FCH // P)[ch]
                         [:, HALF_F * half:HALF_F * (half + 1), :], HALF_F)

            def w1_load(layer):
                if layer:
                    sp.wait_ge(hid_done.sem, hid_done.at(layer - 1, 2))
                for i, name in enumerate(("c_w1_k", "c_w1_v")):
                    sp.dma_start(w1[:, i, :].rearrange("p (a e) -> p a e", e=P),
                                 w[name][layer].rearrange("(a b) d e -> (b d) a e", b=2)).then_inc(w1_landed.sem, 16)

            def aux_loads(layer):
                if layer:
                    sp.wait_ge(ckv_done.sem, ckv_done.at(layer - 1, 2))
                    sp.wait_ge(latup_done.sem, latup_done.at(layer - 1, 4))
                for dst, src in (
                    (w_uq[:, :, :], w["w_uq"][layer].rearrange("(p k) n -> p k n", k=2)),
                    (w_ukv[:, :], w["w_ukv"][layer]),
                    (w2[:, 0, :], w["c_w2_k"][layer]),
                    (w2[:, 1, :], w["c_w2_v"][layer]),
                    (pe_raw[:, 0, :], w["c_pe_k"][layer].rearrange("(a b) d -> a (b d)", b=2)),
                    (pe_raw[:, 1, :], w["c_pe_v"][layer].rearrange("(a b) d -> a (b d)", b=2)),
                ):
                    sp.dma_start(dst, src).then_inc(aux_landed.sem, 16)

            def gpost_load(b):
                name = ("g_post_mix", "g_post_ffn")[b % 2]
                if b:
                    sp.wait_ge(x_updated.sem, x_updated.at(b - 1, NT))
                sp.dma_start(g_post[:, :], bass.AP(w[name].tensor, (b // 2) * D, [[0, P], [1, D]])
                             ).then_inc(gpost_landed.sem, 16)

            for t in range(NT):
                sp.dma_start(x[:, t, :], x_in[0, t * P:(t + 1) * P, :]).then_inc(x_landed.sem, 16)
            sp.wait_ge(con_landed.sem, 16)
            sp.wait_ge(gpre_landed.sem, 32)
            for i in range(RING):
                w_in_piece(0, i)
            aux_loads(0)
            w1_load(0)
            gpost_load(0)
            for i in range(RING, N_W_IN):
                w_in_piece(0, i)
            for i in range(KD // HALF_F):
                w_o_piece(0, i)
            dg, du, dd = w["ffn_w_gate"][0], w["ffn_w_up"][0], w["ffn_w_down"][0]
            up_pieces(DENSE_AT, 0, dg, 0)
            w1_load(1)
            aux_loads(1)
            up_pieces(DENSE_AT + 2, 0, du, 0)
            up_pieces(DENSE_AT + 4, 0, dg, 1)
            gpost_load(1)
            with sp.Fori(1, DCH - 1) as i:
                up_pieces(DENSE_AT, i, du, i)
                down_pieces(DENSE_AT + 2, i, dd, i - 1)
                up_pieces(DENSE_AT + 4, i, dg, i + 1)
            up_pieces(DENSE_AT, DCH - 1, du, DCH - 1)
            down_pieces(DENSE_AT + 2, DCH - 1, dd, DCH - 2)
            down_pieces(DENSE_AT + 4, DCH - 1, dd, DCH - 1)
            for i in range(N_W_IN):
                w_in_piece(1, i)
                if i == RING:
                    gpost_load(2)
            for i in range(KD // HALF_F):
                w_o_piece(1, i)

            def expert_pieces(r, ei, gains=False):
                mg, mu, md = w["moe_w_gate"][0][ei], w["moe_w_up"][0][ei], w["moe_w_down"][0][ei]
                for ch in range(ECH + 1):
                    at = MOE_AT + 6 * ch - 2
                    if ch == 0:
                        up_pieces(MOE_AT, r, mg, 0)
                        up_pieces(MOE_AT + 2, r, mu, 0)
                    elif ch < ECH:
                        up_pieces(at, r, mg, ch)
                        if gains and ch == 1:
                            gpost_load(3)
                        up_pieces(at + 2, r, mu, ch)
                        down_pieces(at + 4, r, md, ch - 1)
                    else:
                        down_pieces(at, r, md, ch - 1)

            expert_pieces(0, 0, gains=True)
            with sp.Fori(1, N_EXP) as e:
                expert_pieces(e * ECH, e)
            sp.wait_ge(over_ready.sem, 1)
            more = sp.value_load(over[0:1, 0:1])
            with sp.If(more > 0):
                with sp.Fori(N_EXP, 2 * N_EXP) as e:
                    expert_pieces(e * ECH, e - N_EXP)
            for t in range(NT):
                sp.wait_ge(x_updated.sem, x_updated.at(3, t + 1))
                sp.dma_start(out[0, t * P:(t + 1) * P, :], x[:, t, :]).then_inc(out_stored.sem, 16)
            sp.wait_ge(out_stored.sem, 16 * NT)

        @block.gpsimd
        def _(pool):
            chain = [0]

            def to_rstd(a, n, stage_in, count, stage_out):
                pool.wait_ge(stage_in.sem, count)
                chain[0] += 1
                pool.tensor_scalar(var[:, a:a + n], mean[:, a:a + n], EPS, None, ALU.add).then_inc(pool_chain.sem, 1)
                pool.wait_ge(pool_chain.sem, chain[0])
                pool.tensor_tensor(rstd[:, a:a + n], var[:, a:a + n], minus_half[:, a:a + n], ALU.pow
                                   ).then_inc(stage_out.sem, 1)

            chain[0] += 1
            pool.memset(minus_half[:, :], -0.5).then_inc(pool_chain.sem, 1)
            pool.wait_ge(pool_chain.sem, 1)
            for layer in range(DEPTH):
                for half in range(2):
                    b = 2 * layer + half
                    for t in range(NT):
                        to_rstd(t, 1, pre_sq, pre_sq.at(b, t + 1), pre_rstd)
                    if half == 0:
                        to_rstd(0, 4, lat_sq, lat_sq.at(layer, 4), lat_rstd)
                        to_rstd(0, 6, o_sq, o_sq.at(layer, 6), o_rstd)
                    for t in range(NT):
                        to_rstd(t, 1, post_sq, post_sq.at(b, t + 1), post_rstd)

        @block.tensor
        def _(pe):
            ident = c("ident")

            def passes(out, lhs, rhs, start, stop):
                pe.matmul(out, lhs[0], rhs[0], start=start, stop=False, skip_group_check=True)
                pe.matmul(out, lhs[0], rhs[1], start=False, stop=False, skip_group_check=True)
                return pe.matmul(out, lhs[1], rhs[0], start=False, stop=stop, skip_group_check=True)

            def piece_view(n, off, dims):
                at = n % SPLITS * PIECE + off
                return view(w_hi, at, dims), view(w_lo, at, dims)

            def turn_h(b):
                for t in range(NT):
                    pe.wait_ge(hn_ready.sem, hn_ready.at(b, t + 1))
                    for half in range(2):
                        for k in range(4):
                            last = pe.transpose(ps[:, 2 * t + half, k * P:(k + 1) * P],
                                                view(zone, HN + t * D + 4 * half + k, [[KD, P]]), ident)
                        last.then_inc(hn_turned.sem, 1)

            def project(layer):
                def begin(i):
                    wait_piece(pe, lo_ready, MIXER_AT[layer] + i, 0)

                def end(last):
                    last.then_inc(piece_used.sem, 1)

                def wcols(i, k, a, n):
                    return piece_view(MIXER_AT[layer] + i, k * (W_IN_CUTS[i + 1] - W_IN_CUTS[i]) + a, [[1, n]])

                def feature_major(bank, col, i, a):
                    for k in range(KD):
                        last = passes(ps[:, bank, col:col + S], wcols(i, k, a, P), (h_hi[:, k, :], h_lo[:, k, :]),
                                      k == 0, k == KD - 1)
                    return last

                def token_major(bank, col, i, a, n, t):
                    for k in range(KD):
                        last = passes(ps[:, bank, col:col + n],
                                      (h_hi[:, k, t * P:(t + 1) * P], h_lo[:, k, t * P:(t + 1) * P]),
                                      wcols(i, k, a, n), k == 0, k == KD - 1)
                    return last

                def keys_values(bank, i):
                    feature_major(bank, 0, i, 0)
                    for t in range(NT):
                        last = token_major(bank, S + t * P, i, P, P, t)
                    return last

                pe.wait_ge(h_ready.sem, h_ready.at(2 * layer, 4))
                begin(0)
                for j in range(2):
                    last = feature_major(0, j * S, 0, j * P)
                end(last)
                begin(1)
                end(keys_values(1, 1))
                for i, col, n in ((2, 0, 256), (3, 256, 160)):
                    begin(i)
                    for t in range(NT):
                        last = token_major(2 + t, col, i, 0, n, t)
                    end(last)
                for g in range(2):
                    begin(4 + g)
                    for j in range(2):
                        last = feature_major(4 + g, j * S, 4 + g, j * P)
                    end(last)
                begin(6)
                for j in range(2):
                    last = feature_major(6, j * S, 6, j * P)
                end(last)
                begin(7)
                pe.wait_ge(proj_out_a.sem, proj_out_a.at(layer, 1))
                end(keys_values(0, 7))
                begin(8)
                pe.wait_ge(proj_out_d.sem, proj_out_d.at(layer, 1))
                end(keys_values(1, 8))
                begin(9)
                pe.wait_ge(proj_out_a.sem, proj_out_a.at(layer, 2))
                for t in range(NT):
                    last = token_major(2, t * 24, 9, 0, 24, t)
                end(last)

            def prepare(layer):
                pe.wait_ge(proj_out_a.sem, proj_out_a.at(layer, 4))
                pe.wait_ge(proj_out_d.sem, proj_out_d.at(layer, 4))
                pe.wait_ge(aux_landed.sem, aux_landed.at(layer + 1, 0))
                for i in range(2):
                    last = pe.transpose(ps[:, 4, i * 16:(i + 1) * 16], pe_raw[:, i, :], ident[0:16, 0:16])
                last.then_inc(pe_turned.sem, 1)
                pe.wait_ge(lat_ready.sem, lat_ready.at(layer, 1))
                for k in range(2):
                    for t in range(NT):
                        last = pe.transpose(ps[:, 3, k * S + t * P:k * S + (t + 1) * P],
                                            view(zone, BL + t * 416 + k, [[2, P]]), ident)
                last.then_inc(lat_turned.sem, 1)
                for t in range(NT):
                    last = pe.transpose(ps[:, 5, t * P:(t + 1) * P], bl[:, t, 256:384], ident)
                last.then_inc(lat_turned.sem, 1)
                pe.wait_ge(latt_ready.sem, latt_ready.at(layer, 2))
                pe.wait_ge(proj_out_d.sem, proj_out_d.at(layer, 6))
                pe.wait_ge(proj_out_a.sem, proj_out_a.at(layer, 7))
                for t in range(NT):
                    for k in range(2):
                        last = pe.matmul(ps[:, (7, 0)[t], 0:384], cqn_t[:, k, t * P:(t + 1) * P], w_uq[:, k, :],
                                         start=(k == 0), stop=(k == 1))
                    last.then_inc(latup_done.sem, 1)
                for t in range(NT):
                    pe.matmul(ps[:, 1 + t, :], cqn_t[:, 2, t * P:(t + 1) * P], w_ukv[:, :],
                              start=True, stop=True).then_inc(latup_done.sem, 1)
                pe.wait_ge(w1_landed.sem, w1_landed.at(layer, 32))
                for i in range(2):
                    pe.wait_ge(blk_ready.sem, blk_ready.at(layer, i + 1))
                    for a in range(16):
                        last = pe.matmul(ps[:, 6, 32 * i:32 * i + 30],
                                         w1[:, i, a * P:(a + 1) * P],
                                         blk[:, i, a * 30:(a + 1) * 30], start=(a == 0), stop=(a == 15))
                    last.then_inc(hid_done.sem, 1)
                pe.wait_ge(qk_ready.sem, qk_ready.at(layer, 1))
                for pair in range(2):
                    for t in range(NT):
                        last = pe.transpose(ps[:, 3, pair * S + t * P:pair * S + (t + 1) * P],
                                            qn[:, t, pair * P:(pair + 1) * P], ident)
                last.then_inc(qk_turned.sem, 1)
                pe.wait_ge(kv_out.sem, kv_out.at(layer, 2))
                for pair in range(2):
                    for t in range(NT):
                        last = pe.transpose(ps[:, 5, pair * S + t * P:pair * S + (t + 1) * P],
                                            kvb[:, t, pair * P:(pair + 1) * P], ident)
                last.then_inc(qk_turned.sem, 1)
                for i in range(2):
                    for t in range(NT):
                        last = pe.transpose(ps[:, 7, i * S + t * P:i * S + (t + 1) * P],
                                            zone[:, ROPE_O + i * S + t * P:ROPE_O + i * S + (t + 1) * P], ident)
                last.then_inc(qk_turned.sem, 1)
                pe.wait_ge(gelu_ready.sem, gelu_ready.at(layer, 1))
                for g in range(2):
                    last = pe.matmul(ps[64 * g:64 * g + 64, 4, 64:64 + N_CMP], w2[:, 0, :],
                                     hid[:, 0, g * 15:g * 15 + 15], start=True, stop=True)
                last.then_inc(ckv_done.sem, 1)
                for i in range(4):
                    for g in range(2):
                        last = pe.matmul(ps[32 * i:32 * i + N_CMP, 4, 128 + g * HEAD:128 + (g + 1) * HEAD],
                                         hid[:, 0, 32 + g * 15:32 + g * 15 + 15], w2[:, 1, :], start=True, stop=True)
                last.then_inc(ckv_done.sem, 1)
                pe.wait_ge(ckv_out.sem, ckv_out.at(layer, 1))
                pe.wait_ge(qk_out.sem, qk_out.at(layer, 3))
                for t in range(NT):
                    for h in range(C_HEADS):
                        g, j = divmod(h, 4)
                        last = pe.matmul(ps[:, 6 + g, (t * 4 + j) * 16:(t * 4 + j) * 16 + N_CMP],
                                         cq_t[64 * g:64 * g + 64, j, t * P:(t + 1) * P],
                                         kc_t[64 * g:64 * g + 64, 0:N_CMP], start=True, stop=True)
                last.then_inc(cs_done.sem, 1)

            def operands(kind, h):
                if kind == "B":
                    half, pair = h % 2, h // 2
                    n, r = slice(64 * half, 64 * half + 64), slice(32 * h, 32 * h + 32)
                    return ([(qn_t[n, pair, :], kn_t[n, pair, :]), (qkr_t[r, 0, :], qkr_t[r, 1, :])],
                            lambda t: kvb[:, t, 256 + h * HEAD:256 + (h + 1) * HEAD])
                g, j = divmod(h, 2 if kind == "A" else 4)
                q = aq_t if kind == "A" else cq_t
                kv = {"A": akv, "S": ksv, "W": kwv}[kind]
                n = slice(64 * g, 64 * g + 64)
                return ([(q[n, j, :], kv[n, 0:S])],
                        lambda t: kv[:, S + t * P + g * HEAD:S + t * P + (g + 1) * HEAD])

            def o_place(kind, h, t):
                if kind in "AB":
                    return ps[:, 4 + (kind == "B"), t * 256 + h * HEAD:t * 256 + (h + 1) * HEAD]
                return ps[:, (6 if kind == "S" else 4) + t, h * HEAD:(h + 1) * HEAD]

            def attention(layer):
                pe.wait_ge(cs_exp.sem, cs_exp.at(layer, 1))
                for t in range(NT):
                    for g in range(2):
                        last = pe.transpose(ps[:, 2, (2 * t + g) * P:(2 * t + g + 1) * P],
                                            view(zone, ROPE_IN + (t * 8 + 4 * g) * 32, [[1, P]]), ident)
                last.then_inc(cp_turned.sem, 1)

                def scores(j):
                    kind, h = JOBS[j]
                    if j >= 2:
                        pe.wait_ge(biased.sem, biased.at(layer, j - 1))
                    pairs, _ = operands(kind, h)
                    for dst, q0, n in ((ps[:, j % 2, 0:P], 0, P), (ps[:, j % 2, P:SPAN], P, S)):
                        for i, (q, k) in enumerate(pairs):
                            last = pe.matmul(dst, q[:, q0:q0 + P], k[:, 0:n], start=(i == 0), stop=(i == len(pairs) - 1))
                    last.then_inc(score_done.sem, 1)

                def turn(j):
                    pe.wait_ge(probs_ready.sem, probs_ready.at(layer, j + 1))
                    if j == 0:
                        pe.wait_ge(cp_out.sem, cp_out.at(layer, 1))
                    elif j >= 2:
                        s = (pt_ready_a, pt_ready_d)[j % 2]
                        pe.wait_ge(s.sem, s.at(layer, j // 2))
                    for b in range(3):
                        last = pe.transpose(ps[:, 2 + j % 2, b * P:(b + 1) * P], sc_sb[:, j % 5, b * P:(b + 1) * P], ident)
                    last.then_inc(probs_turned.sem, 1)

                def values(j):
                    kind, h = JOBS[j]
                    s = (pt_ready_a, pt_ready_d)[j % 2]
                    pe.wait_ge(s.sem, s.at(layer, j // 2 + 1))
                    if (kind, h) == ("S", 0):
                        pe.wait_ge(co_out.sem, co_out.at(layer, 1))
                    if (kind, h) == ("W", 0):
                        pe.wait_ge(o_out.sem, o_out.at(layer, 2))
                    _, v = operands(kind, h)
                    pe.matmul(o_place(kind, h, 0), pt[:, j % 2, 0:P], v(0), start=True, stop=True)
                    pe.matmul(o_place(kind, h, 1), pt[:, j % 2, P:2 * P], v(0), start=True, stop=False)
                    pe.matmul(o_place(kind, h, 1), pt[:, j % 2, 2 * P:SPAN], v(1), start=False, stop=True
                              ).then_inc(pv_done.sem, 1)

                for j in range(NJ + 4):
                    if j < NJ:
                        scores(j)
                    if j == 1:
                        pe.wait_ge(cp_out.sem, cp_out.at(layer, 1))
                        for t in range(NT):
                            for g in range(2):
                                last = pe.matmul(ps[:, 6 + t, g * 256:(g + 1) * 256], pt_cmp[:, 2 * t + g, :],
                                                 v_cmp[:, g, :], start=True, stop=True)
                        last.then_inc(co_done.sem, 1)
                    if 0 <= j - 3 < NJ:
                        turn(j - 3)
                    if 0 <= j - 4 < NJ:
                        values(j - 4)

            def output_projection(layer):
                pe.wait_ge(mixed_ready.sem, mixed_ready.at(layer, 1))
                for t in range(NT):
                    for half in range(2):
                        for k in range(4):
                            last = pe.transpose(ps[:, 2 * t + half, k * P:(k + 1) * P],
                                                view(zone, FO + t * D + 4 * half + k, [[KD, P]]), ident)
                        last.then_inc(mixed_turned.sem, 1)
                pe.wait_ge(mix_ready.sem, mix_ready.at(layer, 4))
                for i in range(KD // HALF_F):
                    n = MIXER_AT[layer] + N_W_IN + i
                    wait_piece(pe, lo_ready, n, 0)
                    for kk in range(HALF_F):
                        k = HALF_F * i + kk
                        for t in range(NT):
                            for half in range(2):
                                last = passes(ps[:, 4 + 2 * t + half, :],
                                              (mix_hi[:, k, t * P:(t + 1) * P], mix_lo[:, k, t * P:(t + 1) * P]),
                                              piece_view(n, kk * D + half * 512, [[1, 512]]), k == 0, k == KD - 1)
                    last.then_inc(piece_used.sem, 1)

            def hidden(n, r, bank, lhs, tiles):
                for half in range(2):
                    wait_piece(pe, lo_ready, n + half, r)
                    for t in range(tiles):
                        for kk in range(HALF_K):
                            k = HALF_K * half + kk
                            last = passes(ps[:, bank + t, :], lhs(k, t),
                                          piece_view(n + half, kk * FCH, [[1, FCH]]), k == 0, k == KD - 1)
                    last.then_inc(piece_used.sem, 1)

            def gate_up(n, r, step, lhs, tiles, first=False):
                if not first:
                    pe.wait_ge(silu_ready.sem, step - 1)
                hidden(n, r, 0, lhs, tiles)
                if not first:
                    pe.wait_ge(act_ready.sem, step - 1)
                hidden(n + 2, r, 2, lhs, tiles)

            def turn(step, tiles):
                pe.wait_ge(prod_ready.sem, step)
                for t in range(tiles):
                    for f in range(FCH // P):
                        last = pe.transpose(ps[:, 2 + t, f * P:(f + 1) * P], sil[:, t, f * P:(f + 1) * P], ident)
                last.then_inc(act_turned.sem, 1)

            def down(n, r, step, tiles, first, last_one):
                pe.wait_ge(act_ready.sem, step)
                for half in range(2):
                    wait_piece(pe, lo_ready, n + half, r)
                    for ff in range(HALF_F):
                        f = HALF_F * half + ff
                        for t in range(tiles):
                            lhs = act_hi[:, t, f * P:(f + 1) * P], act_lo[:, t, f * P:(f + 1) * P]
                            for c2 in range(2):
                                last = passes(ps[:, 4 + 2 * t + c2, :], lhs,
                                              piece_view(n + half, ff * D + c2 * 512, [[1, 512]]),
                                              first and f == 0, last_one and f == FCH // P - 1)
                    last.then_inc(piece_used.sem, 1)

            def dense():
                def tokens(k, t):
                    return h_hi[:, k, t * P:(t + 1) * P], h_lo[:, k, t * P:(t + 1) * P]

                for t in range(NT):
                    for n in range(2):
                        pe.matmul(ps[:, 4 + 2 * t + n, :], zero16[:, 0:P], zero16[:, :], start=True, stop=False,
                                  skip_group_check=True)
                pe.wait_ge(h_ready.sem, h_ready.at(1, 4))
                gate_up(DENSE_AT, 0, 1, tokens, NT, first=True)
                turn(1, NT)
                with pe.Fori(1, DCH) as i:
                    gate_up(DENSE_AT - 2, i, i + 1, tokens, NT)
                    down(DENSE_AT + 2, i, i, NT, False, False)
                    turn(i + 1, NT)
                down(DENSE_AT + 4, DCH - 1, DCH, NT, False, True)

            def route():
                pe.wait_ge(h_ready.sem, h_ready.at(3, 4))
                for t in range(NT):
                    for k in range(KD):
                        for i, h in enumerate((h_hi, h_lo)):
                            last = pe.matmul(ps[:, 6, t * 8:t * 8 + 8], h[:, k, t * P:(t + 1) * P].bitcast(F32),
                                             router[:, k, :], start=(k == 0 and i == 0), stop=(k == KD - 1 and i == 1))
                last.then_inc(logit_done.sem, 1)
                pe.wait_ge(picks_ready.sem, 1)
                mk = rt[:, 2, :]
                pe.matmul(ps[:, 7, 0:8], c("tri"), mk[:, 0:8], start=True, stop=True)
                pe.matmul(ps[:, 7, 8:16], ones[:, :], mk[:, 0:8], start=True, stop=False)
                pe.matmul(ps[:, 7, 8:16], c("tri"), mk[:, 8:16], start=False, stop=True)
                pe.matmul(ps[:, 7, 16:24], ones[:, :], mk[:, 0:8], start=True, stop=False)
                pe.matmul(ps[:, 7, 16:24], ones[:, :], mk[:, 8:16], start=False, stop=True).then_inc(ranks_done.sem, 1)

            def gather(n_sel):
                pe.wait_ge(sel_ready.sem, n_sel)
                for half in range(2):
                    for k in range(4):
                        for t in range(NT):
                            last = pe.matmul(ps[:, 6 + half, k * P:(k + 1) * P],
                                             view(zone, HN + t * D + 4 * half + k, [[KD, P]]), sel[:, t, :],
                                             start=(t == 0), stop=(t == NT - 1))
                    last.then_inc(gathered.sem, 1)

            def expert_up(e, ch):
                if ch == 0:
                    pe.wait_ge(hg_ready.sem, e * 2 + 2)
                gate_up(MOE_AT + (6 * ch - 2 if ch else 0), e * ECH, e * ECH + (DCH + ch + 1),
                        lambda k, t: (hg_hi[:, k, :], hg_lo[:, k, :]), 1)

            def expert_down(e, ch):
                down(MOE_AT + (6 * ch + 8 if ch < ECH - 1 else 6 * ECH - 2), e * ECH, e * ECH + (DCH + ch + 1),
                     1, ch == 0, ch == ECH - 1)

            def expert(e, last_one):
                for ch in range(1, ECH):
                    expert_up(e, ch)
                    expert_down(e, ch - 1)
                    turn(e * ECH + (DCH + ch + 1), 1)
                    if ch == 1:
                        pe.wait_ge(selw_ready.sem, e * 2 + 2)
                        for t in range(NT):
                            last = pe.transpose(ps[:, 6, t * P:(t + 1) * P], sel_w[:, t, :], ident)
                        last.then_inc(selw_turned.sem, 1)
                pe.wait_ge(selwt_ready.sem, e + 1)
                if not last_one:
                    gather(e * 2 + 4)
                expert_down(e, ECH - 1)
                if not last_one:
                    expert_up(e + 1, 0)
                pe.wait_ge(y_ready.sem, e + 1)
                for i in range(4):
                    t, n = divmod(i, 2)
                    if i >= 2:
                        pe.wait_ge(added.sem, e * 4 + (i - 1))
                    pe.matmul(ps[:, 6 + n, :], sel_wt[:, t, :], y_sb[:, n, :], start=True, stop=True
                              ).then_inc(scattered.sem, 1)
                if not last_one:
                    turn(e * ECH + (DCH + ECH + 1), 1)

            def moe_pass(base):
                gather(base * 2 + 2)
                expert_up(base, 0)
                turn(base * ECH + DCH + 1, 1)
                with pe.Fori(base, base + N_EXP - 1) as e:
                    expert(e, False)
                expert(base + N_EXP - 1, True)

            pe.wait_ge(con_landed.sem, 16)
            pe.wait_ge(setup_done.sem, 2)
            for layer in range(DEPTH):
                turn_h(2 * layer)
                project(layer)
                prepare(layer)
                attention(layer)
                output_projection(layer)
                turn_h(2 * layer + 1)
                if layer % 2 == 0:
                    dense()
                else:
                    route()
                    pe.wait_ge(over_ready.sem, 1)
                    moe_pass(0)
            more = pe.value_load(over[0:1, 0:1])
            with pe.If(more > 0):
                pe.wait_ge(added.sem, 4 * N_EXP)
                moe_pass(N_EXP)

        @block.scalar
        def _(act):
            for i, name in enumerate(("g_pre_mix", "g_pre_ffn")):
                act.dma_start(view(g_pre, i * KD, [[2 * KD, DEPTH], [1, KD]]),
                              w[name].rearrange("l (p k) -> p l k", k=KD)).then_inc(gpre_landed.sem, 16)
            act.dma_start(con[:, :], consts_in).then_inc(con_landed.sem, 16)

            def small(dst, src):
                act.dma_start(dst, src).then_inc(small_landed.sem, 16)

            for t in range(NT):
                small(pos_i[:, t:t + 1], pos_in[0, t * P:(t + 1) * P].rearrange("(p o) -> p o", o=1))
            for name, p0, n in (("g_oa", 0, 32), ("g_ob", 32, 32), ("g_oc", 64, 64)):
                small(g_out[p0:p0 + n, :, :], w[name].rearrange("l (p k) -> p l k", k=KD))
            small(g_cq[:, :, :], w["g_cq"].rearrange("l (p k) -> p l k", k=2))
            for layer in range(DEPTH):
                small(g_ckv[:, layer:layer + 1], w["g_ckv"][layer].rearrange("(p o) -> p o", o=1))
            small(sinks[:, :, :], bass.AP(w["a_sinks"].tensor, 0, [[0, P], [1, DEPTH * A_HEADS]]))
            small(router[:, :, :], w["moe_router"][0].rearrange("(p k) e -> p k e", k=KD))

            def square_mean(dst, src, junk, width):
                return act.activation(junk, src, ACT.Square, scale=float(width) ** -0.5, accum_out=dst)

            def split(n, r, words=PIECE):
                act.wait_ge(slot_landed[n % RING].sem, r * 16 + 16 * (n // RING + 1))
                if n >= SPLITS or not isinstance(r, int):
                    wait_piece(act, piece_used, n - SPLITS, r)
                act.activation(w_hi[:, n % SPLITS, 0:words], raw[:, n % RING, 0:words], ACT.Copy
                               ).then_inc(hi_ready.sem, 1)

            def split_w_in(layer, *pieces):
                for i in pieces:
                    split(MIXER_AT[layer] + i, 0, KD * (W_IN_CUTS[i + 1] - W_IN_CUTS[i]))

            def split_rows(gained, hi, dst, b):
                for i in range(4):
                    t, half = divmod(i, 2)
                    act.wait_ge(gained.sem, gained.at(b, i + 1))
                    act.activation(dst[:, 4 * half:4 * half + 4, t * P:(t + 1) * P],
                                   ps[:, i, :].rearrange("p (k n) -> p k n", k=4), ACT.Copy).then_inc(hi.sem, 1)

            def pre_norm(b):
                for t in range(NT):
                    if b == 0:
                        act.wait_ge(x_landed.sem, 16 * NT)
                    else:
                        act.wait_ge(x_updated.sem, x_updated.at(b - 1, t + 1))
                    square_mean(mean[:, t:t + 1], x[:, t, :], hn[:, t, :], D).then_inc(pre_sq.sem, 1)

            def post_norm(b, src):
                for t in range(NT):
                    square_mean(mean[:, t:t + 1], src(t), hn[:, t, :], D).then_inc(post_sq.sem, 1)

            def mixer(layer):
                def copied(i):
                    wait_piece(act, piece_used, MIXER_AT[layer] + i, 0)

                split_w_in(layer, 0, 1, 2)
                split_rows(h_gained, hhi_ready, h_hi, 2 * layer)
                copied(0)
                for h in range(A_HEADS):
                    g, j = divmod(h, 2)
                    last = act.activation(aq_t[64 * g:64 * g + 64, j, :],
                                          ps[64 * (h % 2):64 * (h % 2) + 64, 0, (h // 2) * S:(h // 2 + 1) * S],
                                          ACT.Copy, scale=QK_SCALE)
                last.then_inc(proj_out_a.sem, 1)
                split_w_in(layer, 3, 4, 5)
                copied(3)
                act.activation(bl[:, 0, :], ps[:, 2, 0:416], ACT.Copy).then_inc(proj_out_a.sem, 1)
                act.wait_ge(proj_out_a.sem, proj_out_a.at(layer, 2))
                act.wait_ge(proj_out_d.sem, proj_out_d.at(layer, 2))
                split_w_in(layer, 6)
                for t in range(NT):
                    square_mean(mean[:, 2 * t:2 * t + 1], bl[:, t, 0:256], hn[:, t, 0:256], 256).then_inc(lat_sq.sem, 1)
                    square_mean(mean[:, 2 * t + 1:2 * t + 2], bl[:, t, 256:384], hn[:, t, 256:384], 128
                                ).then_inc(lat_sq.sem, 1)
                if layer == 0:
                    act.wait_ge(sin_ready.sem, 1)
                    act.activation(sincos[:, :, :, :], ang[:, :, :, :], ACT.Sin).then_inc(sin_done.sem, 1)
                for g in range(2):
                    copied(4 + g)
                    act.activation(view(zone, Z + 1024, [[512, 2], [1, S]], 64 * g, 64),
                                   ps[0:64, 4 + g, :].rearrange("p (j n) -> p j n", j=2), ACT.Copy, scale=QK_SCALE
                                   ).then_inc(proj_out_a.sem, 1)
                    split_w_in(layer, 7 + g)
                copied(6)
                for g in range(2):
                    last = act.activation(view(zone, XS + g * S, [[512, 2], [1, S]], 0, 64),
                                          ps[64 * g:64 * g + 64, 6, :].rearrange("p (i n) -> p i n", i=2), ACT.Copy)
                last.then_inc(proj_out_a.sem, 1)
                split_w_in(layer, 9)
                copied(7)
                act.activation(ksv, ps[:, 0, :], ACT.Copy).then_inc(proj_out_a.sem, 1)
                copied(9)
                act.activation(gate[:, :, :], ps[:, 2, 0:48].rearrange("p (t n) -> p t n", t=NT), ACT.Exp, scale=-1.0
                               ).then_inc(proj_out_a.sem, 1)
                for t in range(NT):
                    act.wait_ge(latup_done.sem, latup_done.at(layer, 3 + t))
                    act.activation(view(zone, CQN + 1280 + t * 512, [[64, 4], [256, 2], [1, 64]]),
                                   ps[:, 1 + t, :].rearrange("p (h i d) -> p h i d", h=4, i=2), ACT.Copy
                                   ).then_inc(kv_out.sem, 1)
                act.wait_ge(gelu_arg.sem, gelu_arg.at(layer, 1))
                act.activation(hid[:, 2, 0:62], hid[:, 1, 0:62], ACT.Exp, scale=-GELU_C).then_inc(gelu_exp.sem, 1)
                for i, bank in ((0, 3), (1, 5), (2, 7)):
                    act.wait_ge(qk_turned.sem, qk_turned.at(layer, i + 1))
                    act.activation(zv(QN_T + 512 * i, 512), ps[:, bank, :], ACT.Copy).then_inc(qk_out.sem, 1)
                act.wait_ge(cs_arg.sem, cs_arg.at(layer, 1))
                act.activation(p_cmp[:, :, 0:N_CMP], p_cmp[:, :, 0:N_CMP], ACT.Exp).then_inc(cs_exp.sem, 1)

                w_o_at = MIXER_AT[layer] + N_W_IN
                for j in range(NJ + 3):
                    if j < NJ:
                        act.wait_ge(max_ready.sem, max_ready.at(layer, j + 1))
                        act.activation(sc_sb[:, j % 5, 0:P], sc_sb[:, j % 5, 0:P], ACT.Exp, bias=nmax[:, j, 0:1],
                                       accum_out=rsum[:, j, 0:1])
                        act.activation(sc_sb[:, j % 5, P:SPAN], sc_sb[:, j % 5, P:SPAN], ACT.Exp, bias=nmax[:, j, 1:2],
                                       accum_out=rsum[:, j, 1:2]).then_inc(probs_ready.sem, 1)
                    if j == 5:
                        act.wait_ge(sink_arg.sem, sink_arg.at(layer, 1))
                        act.activation(sink_e[:, :, :], sink_e[:, :, :], ACT.Exp).then_inc(sink_exp.sem, 1)
                    i = j - 3
                    if i >= 0 and i < NJ and i % 2 == 0:
                        act.wait_ge(probs_turned.sem, probs_turned.at(layer, i + 1))
                        if i >= 2:
                            act.wait_ge(pv_done.sem, pv_done.at(layer, i - 1))
                        act.activation(pt[:, 0, :], ps[:, 2, 0:SPAN], ACT.Copy).then_inc(pt_ready_a.sem, 1)
                    if j in (8, 12, 16):
                        split(w_o_at + (j - 8) // 4, 0)
                act.wait_ge(o_out.sem, o_out.at(layer, 4))
                for t in range(NT):
                    for g, (a, n) in enumerate(((0, 256), (256, 256), (512, 512))):
                        square_mean(mean[:, 3 * t + g:3 * t + g + 1], o_all[:, t, a:a + n], hn[:, t, a:a + n], n
                                    ).then_inc(o_sq.sem, 1)
                split_rows(mix_gained, mixhi_ready, mix_hi, layer)
                for i in range(3, 6):
                    split(w_o_at + i, 0)
                wait_piece(act, piece_used, w_o_at + 3, 0)
                act.wait_ge(mixed_ready.sem, mixed_ready.at(layer, 1))
                post_norm(2 * layer, lambda t: ps[:, 4 + 2 * t:6 + 2 * t, :])

            def silu(n, r, step, tiles, first=False):
                wait_piece(act, piece_used, n, r)
                if not first:
                    act.wait_ge(act_turned.sem, step - 1)
                act.activation(sil[:, 0:tiles, :], ps[:, 0:tiles, :], ACT.Silu).then_inc(silu_ready.sem, 1)

            def split_act(step, tiles):
                act.wait_ge(act_turned.sem, step)
                act.activation(act_hi[:, 0:tiles, :], ps[:, 2:2 + tiles, :], ACT.Copy).then_inc(acthi_ready.sem, 1)

            def chunk(at, r, step, tiles, tail=6):
                split(at + 4, r)
                silu(at + 1, r, step, tiles)
                for i in (5, 6, 7):
                    if i < tail:
                        split(at + i, r)
                split_act(step, tiles)
                for i in (8, 9):
                    if i < tail:
                        split(at + i, r)

            for layer in range(DEPTH):
                pre_norm(2 * layer)
                mixer(layer)
                pre_norm(2 * layer + 1)
                b0 = (DENSE_AT, MOE_AT)[layer]
                split(b0 + 2, 0)
                split_rows(h_gained, hhi_ready, h_hi, 2 * layer + 1)
                if layer % 2 == 0:
                    split(DENSE_AT + 3, 0)
                    split(DENSE_AT + 4, 0)
                    silu(DENSE_AT + 1, 0, 1, NT, first=True)
                    split(DENSE_AT + 5, 0)
                    split(DENSE_AT + 6, 0)
                    split_act(1, NT)
                    split(DENSE_AT + 7, 0)
                    with act.Fori(1, DCH - 1) as i:
                        chunk(DENSE_AT - 2, i, i + 1, NT, tail=10)
                    chunk(DENSE_AT - 2, DCH - 1, DCH, NT, tail=8)
                    wait_piece(act, piece_used, DENSE_AT + 6 * DCH - 1, 0)
                    post_norm(1, lambda t: ps[:, 4 + 2 * t:6 + 2 * t, :])
                else:
                    act.wait_ge(route_arg.sem, 1)
                    act.activation(rt[:, 10, 0:2], rt[:, 9, 0:2], ACT.Exp).then_inc(route_exp.sem, 1)

            def split_gathered(e):
                for half in range(2):
                    act.wait_ge(hg_gained.sem, e * 2 + (half + 1))
                    act.activation(hg_hi[:, 4 * half:4 * half + 4, :],
                                   ps[:, 6 + half, :].rearrange("p (k n) -> p k n", k=4), ACT.Copy
                                   ).then_inc(hghi_ready.sem, 1)

            def expert(e, last_one):
                r = e * ECH
                for ch in range(1, ECH - 1):
                    chunk(MOE_AT + 6 * ch - 2, r, e * ECH + (DCH + ch + 1), 1, tail=10)
                at, step = MOE_AT + 6 * ECH - 8, e * ECH + (DCH + ECH)
                chunk(at, r, step, 1, tail=8)
                if not last_one:
                    split_gathered(e + 1)
                    for i in (8, 9, 10):
                        split(at + i, r)
                wait_piece(act, piece_used, at + 7, r)
                act.activation(y_sb, ps[:, 4:6, :], ACT.Copy).then_inc(y_ready.sem, 1)
                if not last_one:
                    split(at + 11, r)
                    split(at + 12, r)
                    silu(at + 9, r, e * ECH + (DCH + ECH + 1), 1)
                    split(at + 13, r)
                    split(at + 14, r)
                    split_act(e * ECH + (DCH + ECH + 1), 1)
                    split(at + 15, r)

            def moe_pass(base, second):
                r, step = base * ECH, base * ECH + DCH + 1
                if second:
                    for i in range(3):
                        split(MOE_AT + i, r)
                split_gathered(base)
                for i in (3, 4):
                    split(MOE_AT + i, r)
                silu(MOE_AT + 1, r, step, 1)
                for i in (5, 6):
                    split(MOE_AT + i, r)
                split_act(step, 1)
                split(MOE_AT + 7, r)
                with act.Fori(base, base + N_EXP - 1) as e:
                    expert(e, False)
                expert(base + N_EXP - 1, True)

            moe_pass(0, False)
            act.wait_ge(over_ready.sem, 1)
            more = act.value_load(over[0:1, 0:1])
            with act.If(more > 0):
                moe_pass(N_EXP, True)
            act.wait_ge(f_summed.sem, 1)
            post_norm(3, lambda t: f_acc[:, t, :])

        @block.vector
        def _(dve):
            chain = [0]

            def link(ins):
                chain[0] += 1
                ins.then_inc(dve_chain.sem, 1)
                dve.wait_ge(dve_chain.sem, chain[0])

            def rest(n, r, words=PIECE):
                wait_piece(dve, hi_ready, n, r)
                dve.tensor_tensor(w_lo[:, n % SPLITS, 0:words], raw[:, n % RING, 0:words],
                                  w_hi[:, n % SPLITS, 0:words].bitcast(F32), ALU.subtract).then_inc(lo_ready.sem, 1)

            def rest_rows(turned, gained, hi_in, ready, lo, hi, gain, b):
                def place(i):
                    t, half = divmod(i, 2)
                    return (t, half, ps[:, i, :].rearrange("p (k n) -> p k n", k=4))

                def times_gain(i):
                    t, half, at = place(i)
                    dve.wait_ge(turned.sem, turned.at(b, i + 1))
                    dve.tensor_tensor(at, at, view(gain, b * KD + 4 * half, [[1, 4], [0, P]]), ALU.mult
                                      ).then_inc(gained.sem, 1)

                times_gain(0)
                for i in range(4):
                    if i < 3:
                        times_gain(i + 1)
                    t, half, at = place(i)
                    dve.wait_ge(hi_in.sem, hi_in.at(b, i + 1))
                    part = (slice(None), slice(4 * half, 4 * half + 4), slice(t * P, (t + 1) * P))
                    dve.tensor_tensor(lo[part], at, hi[part].bitcast(F32), ALU.subtract).then_inc(ready.sem, 1)

            def pre_norm(b, pieces):
                for t in range(NT):
                    dve.wait_ge(pre_rstd.sem, pre_rstd.at(b, t + 1))
                    dve.tensor_scalar(hn[:, t, :], x[:, t, :], rstd[:, t:t + 1], None, ALU.mult
                                      ).then_inc(hn_ready.sem, 1)
                for n, words in pieces:
                    rest(n, 0, words)
                rest_rows(hn_turned, h_gained, hhi_ready, h_ready, h_lo, h_hi, g_pre, b)

            def post_norm(b, src):
                dve.wait_ge(gpost_landed.sem, gpost_landed.at(b, 16))
                for t in range(NT):
                    dve.wait_ge(post_rstd.sem, post_rstd.at(b, t + 1))
                    hv = hn[:, t, :].rearrange("p (n c) -> p n c", n=2)
                    link(dve.scalar_tensor_tensor(out=hv, in0=src(t), scalar=rstd[:, t:t + 1],
                                                  in1=g_post[:, :].rearrange("p (n c) -> p n c", n=2),
                                                  op0=ALU.mult, op1=ALU.mult))
                    dve.tensor_tensor(x[:, t, :], x[:, t, :], hn[:, t, :], ALU.add).then_inc(x_updated.sem, 1)

            def mixer(layer):
                def projected(i):
                    wait_piece(dve, piece_used, MIXER_AT[layer] + i, 0)

                def rest_w_in(i):
                    rest(MIXER_AT[layer] + i, 0, KD * (W_IN_CUTS[i + 1] - W_IN_CUTS[i]))

                rest_w_in(2)
                if layer == 0:
                    dve.wait_ge(small_landed.sem, 16 * N_SMALL)
                    rotary_setup()
                rest_w_in(3)
                projected(1)
                dve.tensor_copy(akv, ps[:, 1, :]).then_inc(proj_out_d.sem, 1)
                rest_w_in(4)
                rest_w_in(5)
                projected(3)
                dve.tensor_copy(bl[:, 1, :], ps[:, 3, 0:416]).then_inc(proj_out_d.sem, 1)
                rest_w_in(6)
                for g in range(2):
                    projected(4 + g)
                    dve.tensor_scalar(view(zone, Z + 1024 + 256, [[512, 2], [1, S]], 64 * g, 64),
                                      ps[64:128, 4 + g, :].rearrange("p (j n) -> p j n", j=2), QK_SCALE, None, ALU.mult
                                      ).then_inc(proj_out_d.sem, 1)
                    rest_w_in(7 + g)
                dve.wait_ge(lat_rstd.sem, lat_rstd.at(layer, 1))
                for t in range(NT):
                    for i, (a, n) in enumerate(((0, 256), (256, 128))):
                        last = dve.tensor_scalar(bl[:, t, a:a + n], bl[:, t, a:a + n], rstd[:, 2 * t + i:2 * t + i + 1],
                                                 None, ALU.mult)
                last.then_inc(lat_ready.sem, 1)
                rest_w_in(9)
                dve.wait_ge(pe_turned.sem, pe_turned.at(layer, 1))
                link(dve.tensor_copy(pe_t[:, :, :], ps[:, 4, 0:32].rearrange("p (i a) -> p i a", i=2)))
                projected(6)
                dve.wait_ge(proj_out_a.sem, proj_out_a.at(layer, 5))
                for g in range(2):
                    last = dve.tensor_copy(view(zone, XS + g * S, [[512, 2], [1, 255]], 64, 64),
                                           view(ps, 6 * 512 + 1, [[256, 2], [1, 255]], 64 * g, 64))
                last.then_inc(proj_out_d.sem, 1)
                dve.wait_ge(proj_out_d.sem, proj_out_d.at(layer, 5))
                dve.wait_ge(lat_sq.sem, lat_sq.at(layer, 4))
                for i in range(2):
                    for g in range(2):
                        last = dve.tensor_tensor(view(zone, HN + i * 480 + g * 15, [[30, 16], [1, 15]]),
                                                 view(zone, XS + i * 512 + g * 256, [[2, 16], [16, 15]]),
                                                 view(pe_t, i * 16, [[1, 16], [0, 15]]), ALU.add)
                    last.then_inc(blk_ready.sem, 1)
                for i, (bank, n) in enumerate(((3, 2), (5, 1))):
                    dve.wait_ge(lat_turned.sem, lat_turned.at(layer, i + 1))
                    if i == 0:
                        dve.tensor_tensor(cqn_t[:, 0:2, :], ps[:, 3, :].rearrange("p (k n) -> p k n", k=2),
                                          view(g_cq, layer * 2, [[1, 2], [0, S]]), ALU.mult).then_inc(latt_ready.sem, 1)
                    else:
                        dve.tensor_scalar(cqn_t[:, 2, :], ps[:, 5, 0:S], g_ckv[:, layer:layer + 1], None, ALU.mult
                                          ).then_inc(latt_ready.sem, 1)
                projected(8)
                dve.tensor_copy(kwv, ps[:, 1, :]).then_inc(proj_out_d.sem, 1)
                dve.wait_ge(proj_out_a.sem, proj_out_a.at(layer, 7))
                link(dve.tensor_scalar(gate[:, :, :], gate[:, :, :], 1.0, None, ALU.add))
                link(dve.reciprocal(gate[:, :, :], gate[:, :, :]))
                if layer == 0:
                    dve.wait_ge(sin_done.sem, 1)
                for t in range(NT):
                    dve.wait_ge(latup_done.sem, latup_done.at(layer, t + 1))
                    bank = (7, 0)[t]
                    dve.tensor_copy(view(zone, CQN + 768 + t * 256, [[64, 4], [1, 64]]),
                                    view(ps, bank * 512, [[96, 4], [1, 64]]))
                    dve.tensor_copy(view(zone, ROPE_IN + t * 160, [[32, 4], [1, 32]]),
                                    view(ps, bank * 512 + 64, [[96, 4], [1, 32]])).then_inc(latup_out.sem, 1)
                    link(dve.tensor_copy(view(zone, ROPE_IN + t * 160 + 128, [[1, 32]]), bl[:, t, 384:416]))
                    rope_in = view(zone, ROPE_IN + t * 160, [[32, 5], [16, 2], [1, 16]])
                    cos = view(sincos, 32 + t * 16, [[0, 5], [0, 2], [1, 16]])
                    sin = view(sincos, t * 16, [[0, 5], [0, 2], [1, 16]])
                    dve.tensor_tensor(view(zone, ROPE_A + t * 160, [[32, 5], [16, 2], [1, 16]]), rope_in, cos, ALU.mult)
                    link(dve.tensor_tensor(view(zone, ROPE_B + t * 160, [[32, 5], [16, 2], [1, 16]]), rope_in, sin,
                                           ALU.mult))
                    for half, op in ((0, ALU.subtract), (1, ALU.add)):
                        dve.tensor_tensor(view(zone, ROPE_O + t * P + half * 16, [[32, 4], [1, 16]]),
                                          view(zone, ROPE_A + t * 160 + half * 16, [[32, 4], [1, 16]]),
                                          view(zone, ROPE_B + t * 160 + (1 - half) * 16, [[32, 4], [1, 16]]), op)
                        last = dve.tensor_tensor(view(zone, ROPE_O + S + t * P + half * 16, [[32, 4], [1, 16]]),
                                                 view(zone, ROPE_A + t * 160 + 128 + half * 16, [[0, 4], [1, 16]]),
                                                 view(zone, ROPE_B + t * 160 + 128 + (1 - half) * 16, [[0, 4], [1, 16]]),
                                                 op)
                last.then_inc(qk_ready.sem, 1)
                dve.wait_ge(qk_ready.sem, qk_ready.at(layer, 1))
                link(dve.memset(p_cmp, 0.0))
                dve.wait_ge(hid_done.sem, hid_done.at(layer, 2))
                link(dve.tensor_copy(hid[:, 0, 0:62], ps[:, 6, 0:62]))
                link(dve.tensor_tensor(hid[:, 1, 0:62], hid[:, 0, 0:62], hid[:, 0, 0:62], ALU.mult))
                link(dve.tensor_scalar(hid[:, 1, 0:62], hid[:, 1, 0:62], 0.044715, 1.0, ALU.mult, ALU.add))
                dve.tensor_tensor(hid[:, 1, 0:62], hid[:, 1, 0:62], hid[:, 0, 0:62], ALU.mult).then_inc(gelu_arg.sem, 1)
                dve.wait_ge(gelu_exp.sem, gelu_exp.at(layer, 1))
                link(dve.tensor_scalar(hid[:, 2, 0:62], hid[:, 2, 0:62], 1.0, None, ALU.add))
                link(dve.reciprocal(hid[:, 3, 0:62], hid[:, 2, 0:62]))
                dve.tensor_tensor(hid[:, 0, 0:62], hid[:, 0, 0:62], hid[:, 3, 0:62], ALU.mult
                                  ).then_inc(gelu_ready.sem, 1)
                dve.wait_ge(ckv_done.sem, ckv_done.at(layer, 2))
                dve.tensor_copy(kc_t[:, 0:N_CMP], ps[:, 4, 64:64 + N_CMP])
                for i in range(4):
                    last = dve.tensor_copy(v_cmp[32 * i:32 * i + N_CMP, :, HEAD * i:HEAD * (i + 1)],
                                           ps[32 * i:32 * i + N_CMP, 4, 128:256].rearrange("p (g d) -> p g d", g=2))
                last.then_inc(ckv_out.sem, 1)
                dve.wait_ge(cs_done.sem, cs_done.at(layer, 1))
                for h in range(C_HEADS):
                    last = dve.scalar_tensor_tensor(out=view(zone, ROPE_IN + h * 32, [[256, NT], [1, N_CMP]]),
                                                    in0=c("dist_cmp").rearrange("p (t n) -> p t n", t=NT),
                                                    scalar=C_SLOPES[h],
                                                    in1=view(ps, (6 + h // 4) * 512 + h % 4 * 16, [[64, NT], [1, N_CMP]]),
                                                    op0=ALU.mult, op1=ALU.add)
                link(last)
                link(dve.tensor_reduce(cmax[:, :], p_cmp[:, :, 0:N_CMP], AX_X, ALU.max, negate=True))
                dve.tensor_tensor(p_cmp[:, :, 0:N_CMP], p_cmp[:, :, 0:N_CMP], view(cmax, 0, [[1, 16], [0, N_CMP]]), ALU.add
                                  ).then_inc(cs_arg.sem, 1)

                def gated(branch, r, first):
                    for t in range(NT):
                        g = view(gate, t * 24 + branch, [[3, 8]])
                        if first:
                            a, _ = COL["has_cmp"]
                            link(dve.scalar_tensor_tensor(out=gscale[:, t, :], in0=r(t), scalar=con[:, a + t:a + t + 1],
                                                          in1=g, op0=ALU.mult, op1=ALU.mult))
                        else:
                            link(dve.tensor_tensor(gscale[:, t, :], r(t), g, ALU.mult))
                    for t in range(NT):
                        src = ps[:, (4 if branch == 2 else 6) + t, :].rearrange("p (h d) -> p h d", h=8)
                        fac = view(gscale, t * 8, [[1, 8], [0, HEAD]])
                        dst = o_all[:, t, 512:1024]
                        if first:
                            last = dve.tensor_tensor(dst.rearrange("p (h d) -> p h d", h=8), src, fac, ALU.mult)
                        else:
                            link(dve.tensor_tensor(c_tmp.rearrange("p (h d) -> p h d", h=8), src, fac, ALU.mult))
                            last = dve.tensor_tensor(dst, dst, c_tmp, ALU.add)
                            if t == 0:
                                link(last)
                    return last

                def copy_o(kind, j0):
                    for t in range(NT):
                        bank, col = (4, 0) if kind == "A" else (5, 256)
                        last = dve.tensor_tensor(o_all[:, t, col:col + 256].rearrange("p (h d) -> p h d", h=4),
                                                 ps[:, bank, t * 256:(t + 1) * 256].rearrange("p (h d) -> p h d", h=4),
                                                 view(rinv, j0 * 2 + t, [[2, 4], [0, HEAD]]), ALU.mult)
                    return last

                w_o_at = MIXER_AT[layer] + N_W_IN
                for j in range(NJ + 3):
                    if j < NJ:
                        kind, h = JOBS[j]
                        dve.wait_ge(score_done.sem, score_done.at(layer, j + 1))
                        if j >= 5:
                            dve.wait_ge(probs_turned.sem, probs_turned.at(layer, j - 4))
                        s = sc_sb[:, j % 5, :]
                        raw = ps[:, j % 2, 0:SPAN]
                        if kind == "B":
                            ins = dve.scalar_tensor_tensor(out=s, in0=raw, scalar=B_SCALE, in1=c("mask_b"),
                                                           op0=ALU.mult, op1=ALU.add)
                        else:
                            ins = dve.scalar_tensor_tensor(out=s, in0=c("dist_a" if kind == "A" else "dist_c"),
                                                           scalar=(A_SLOPES if kind == "A" else C_SLOPES)[h],
                                                           in1=raw, op0=ALU.mult, op1=ALU.add)
                        ins.then_inc(biased.sem, 1)
                        dve.wait_ge(biased.sem, biased.at(layer, j + 1))
                        dve.tensor_reduce(nmax[:, j, 0:1], s[:, 0:P], AX_X, ALU.max, negate=True)
                        ins = dve.tensor_reduce(nmax[:, j, 1:2], s[:, P:SPAN], AX_X, ALU.max, negate=True)
                        if kind == "A":
                            link(ins)
                            ins = dve.tensor_scalar(nmax[:, j, :], nmax[:, j, :], neg_sinks[:, layer, h:h + 1], None,
                                                    ALU.min)
                        ins.then_inc(max_ready.sem, 1)
                    i = j - 3
                    if i >= 0 and i < NJ and i % 2 == 1:
                        dve.wait_ge(probs_turned.sem, probs_turned.at(layer, i + 1))
                        if i >= 2:
                            dve.wait_ge(pv_done.sem, pv_done.at(layer, i - 1))
                        dve.tensor_copy(pt[:, 1, :], ps[:, 3, 0:SPAN]).then_inc(pt_ready_d.sem, 1)
                    if j == 0:
                        dve.wait_ge(cp_turned.sem, cp_turned.at(layer, 1))
                        dve.tensor_copy(pt_cmp, ps[:, 2, :].rearrange("p (a b) -> p a b", b=P)).then_inc(cp_out.sem, 1)
                        link(dve.tensor_reduce(csum[:, :], p_cmp[:, :, 0:N_CMP], AX_X, ALU.add))
                        link(dve.reciprocal(csum[:, :], csum[:, :]))
                    if j == 2:
                        dve.wait_ge(co_done.sem, co_done.at(layer, 1))
                        gated(0, lambda t: csum[:, t * 8:t * 8 + 8], True).then_inc(co_out.sem, 1)
                    if j == 4:
                        dve.wait_ge(max_ready.sem, max_ready.at(layer, 4))
                        dve.tensor_tensor(sink_e[:, :, :], nmax[:, 0:4, :], view(sinks, layer * 4, [[1, 4], [0, 2]]), ALU.add
                                          ).then_inc(sink_arg.sem, 1)
                    if j == 9:
                        dve.wait_ge(sink_exp.sem, sink_exp.at(layer, 1))
                        link(dve.tensor_tensor(rsum[:, 0:4, :], rsum[:, 0:4, :], sink_e[:, :, :], ALU.add))
                        link(dve.reciprocal(rinv[:, 0:4, :], rsum[:, 0:4, :]))
                        dve.wait_ge(pv_done.sem, pv_done.at(layer, 4))
                        copy_o("A", 0).then_inc(o_out.sem, 1)
                    if j == 12:
                        rest(w_o_at, 0)
                    if j == 13:
                        dve.wait_ge(pv_done.sem, pv_done.at(layer, 8))
                        link(dve.reciprocal(rinv[:, 4:8, :], rsum[:, 4:8, :]))
                        copy_o("B", 4).then_inc(o_out.sem, 1)
                    if j == 21:
                        dve.wait_ge(pv_done.sem, pv_done.at(layer, 16))
                        link(dve.reciprocal(rinv[:, 8:16, :], rsum[:, 8:16, :]))
                        gated(1, lambda t: view(rinv, 16 + t, [[2, 8]]), False).then_inc(o_out.sem, 1)
                dve.wait_ge(o_out.sem, o_out.at(layer, 3))
                dve.wait_ge(pv_done.sem, pv_done.at(layer, NJ))
                link(dve.reciprocal(rinv[:, 16:24, :], rsum[:, 16:24, :]))
                gated(2, lambda t: view(rinv, 32 + t, [[2, 8]]), False).then_inc(o_out.sem, 1)
                rest(w_o_at + 1, 0)
                rest(w_o_at + 2, 0)
                dve.wait_ge(o_rstd.sem, o_rstd.at(layer, 1))
                for t in range(NT):
                    for g, (a, n) in enumerate(((0, 256), (256, 256), (512, 512))):
                        last = dve.tensor_scalar(o_all[:, t, a:a + n], o_all[:, t, a:a + n],
                                                 rstd[:, 3 * t + g:3 * t + g + 1], None, ALU.mult)
                last.then_inc(mixed_ready.sem, 1)
                rest_rows(mixed_turned, mix_gained, mixhi_ready, mix_ready, mix_lo, mix_hi, g_out, layer)
                for i in range(3, 6):
                    rest(w_o_at + i, 0)
                post_norm(2 * layer, lambda t: ps[:, 4 + 2 * t:6 + 2 * t, :])

            def product(n, r, step, tiles):
                wait_piece(dve, piece_used, n, r)
                dve.wait_ge(silu_ready.sem, step)
                dve.tensor_tensor(sil[:, 0:tiles, :], sil[:, 0:tiles, :], ps[:, 2:2 + tiles, :], ALU.mult
                                  ).then_inc(prod_ready.sem, 1)

            def rest_act(step, tiles):
                dve.wait_ge(acthi_ready.sem, step)
                dve.tensor_tensor(act_lo[:, 0:tiles, :], ps[:, 2:2 + tiles, :],
                                  act_hi[:, 0:tiles, :].bitcast(F32), ALU.subtract).then_inc(act_ready.sem, 1)

            def chunk(at, r, step, tiles, tail=12):
                product(at + 3, r, step, tiles)
                for i in (6, 7):
                    rest(at + i, r)
                rest_act(step, tiles)
                for i in range(8, tail):
                    rest(at + i, r)

            def setup():
                dve.memset(ones[:, :], 1.0)
                dve.memset(zero16[:, :], 0.0).then_inc(setup_done.sem, 1)
                dve.memset(v_cmp[:, :, :], 0.0).then_inc(setup_done.sem, 1)

            def rotary_setup():
                link(dve.tensor_copy(pos_f[:, :], pos_i[:, :]))
                dve.tensor_scalar(neg_sinks[:, :, :], sinks[:, :, :], -1.0, None, ALU.mult)
                for t in range(NT):
                    for i in range(2):
                        last = dve.tensor_scalar(ang[:, i, t, :], c("inv_freq"), pos_f[:, t:t + 1], None, ALU.mult)
                link(last)
                dve.tensor_scalar(turns[:, 0, :, :], ang[:, 0, :, :], 1.0 / TWO_PI, None, ALU.mult)
                link(dve.tensor_scalar(turns[:, 1, :, :], ang[:, 1, :, :], 1.0 / TWO_PI, 0.25, ALU.mult, ALU.add))
                link(dve.tensor_scalar(turns[:, :, :, :], turns[:, :, :, :], ROUND, None, ALU.add))
                link(dve.tensor_scalar(turns[:, :, :, :], turns[:, :, :, :], ROUND, None, ALU.subtract))
                a2, t2 = (v[:, :, :, :].rearrange("p a t n -> p (a t n)") for v in (ang, turns))
                for part in (PI_1, PI_2, PI_3):
                    link(dve.scalar_tensor_tensor(out=a2, in0=t2, scalar=-part, in1=a2, op0=ALU.mult, op1=ALU.add))
                link(dve.tensor_scalar(ang[:, 1, :, :], ang[:, 1, :, :], float(np.pi / 2), None, ALU.add))
                dve.tensor_scalar(a2, a2, SIN_MAX, -SIN_MAX, ALU.min, ALU.max).then_inc(sin_ready.sem, 1)

            def pick(logits, scratch, chosen, top):
                link(dve.tensor_reduce(top, logits, AX_X, ALU.max))
                topb = bass.AP(top.tensor, top.offset, [list(top.ap[0]), list(top.ap[1]), [0, 8]])
                link(dve.tensor_tensor(scratch, logits, topb, ALU.is_ge))
                a, _ = COL["iota"]
                iota8 = view(con, a, [[0, NT], [1, 8]])
                link(dve.tensor_scalar(scratch, scratch, -8.0, 8.0, ALU.mult, ALU.add))
                link(dve.tensor_tensor(scratch, scratch, iota8, ALU.add))
                link(dve.tensor_reduce(cnt[:, 0:2], scratch, AX_X, ALU.min))
                link(dve.tensor_tensor(chosen, iota8, view(cnt, 0, [[1, NT], [0, 8]]), ALU.is_equal))

            def route():
                def r(i):
                    return rt[:, i, :].rearrange("p (t e) -> p t e", t=NT)

                dve.wait_ge(logit_done.sem, 1)
                link(dve.tensor_copy(rt[:, 0, :], ps[:, 6, 0:16]))
                m1, m2 = rt[:, 7, 0:2], rt[:, 8, 0:2]
                pick(r(0), r(5), r(3), m1)
                link(dve.scalar_tensor_tensor(out=rt[:, 1, :], in0=rt[:, 3, :], scalar=-1e38, in1=rt[:, 0, :],
                                              op0=ALU.mult, op1=ALU.add))
                pick(r(1), r(5), r(4), m2)
                link(dve.tensor_tensor(rt[:, 2, :], rt[:, 3, :], rt[:, 4, :], ALU.add))
                dve.tensor_tensor(rt[:, 9, 0:2], m2, m1, ALU.subtract).then_inc(route_arg.sem, 1)
                dve.engine_nop().then_inc(picks_ready.sem, 1)
                dve.wait_ge(route_exp.sem, 1)
                link(dve.tensor_scalar(rt[:, 9, 2:4], rt[:, 10, 0:2], 1.0, None, ALU.add))
                link(dve.reciprocal(rt[:, 9, 4:6], rt[:, 9, 2:4]))
                link(dve.tensor_tensor(rt[:, 9, 6:8], rt[:, 9, 4:6], rt[:, 10, 0:2], ALU.mult))
                link(dve.tensor_tensor(r(3), r(3), view(rt, 9 * 16 + 4, [[1, NT], [0, 8]]), ALU.mult))
                link(dve.tensor_tensor(r(4), r(4), view(rt, 9 * 16 + 6, [[1, NT], [0, 8]]), ALU.mult))
                link(dve.tensor_tensor(rt[:, 5, :], rt[:, 3, :], rt[:, 4, :], ALU.add))
                dve.wait_ge(ranks_done.sem, 1)
                link(dve.tensor_tensor(rt[:, 6, :], ps[:, 7, 0:16], rt[:, 2, :], ALU.mult))
                link(dve.tensor_scalar(rt[:, 6, :], rt[:, 6, :], -1.0, None, ALU.add))
                link(dve.tensor_reduce(cnt[:, 0:1], ps[:, 7, 16:24], AX_X, ALU.max))
                dve.tensor_scalar(over[:, :], cnt[:, 0:1], float(P), None, ALU.is_gt).then_inc(over_ready.sem, 1)

            def select(e):
                for t in range(NT):
                    dve.tensor_scalar(sel[:, t, :], c("iota"), rt[:, 6, bass.ds(e + t * 8, 1)], None, ALU.is_equal
                                      ).then_inc(sel_ready.sem, 1)

            def expert(e, ei, last_one):
                r = e * ECH
                for t in range(NT):
                    dve.tensor_scalar(sel_w[:, t, :], c("iota"), rt[:, 6, bass.ds(ei + t * 8, 1)],
                                      rt[:, 5, bass.ds(ei + t * 8, 1)], ALU.is_equal, ALU.mult).then_inc(selw_ready.sem, 1)
                if not last_one:
                    select(ei + 1)
                for ch in range(1, ECH - 1):
                    chunk(MOE_AT + 6 * ch - 2, r, e * ECH + (DCH + ch + 1), 1)
                    if ch == 1:
                        dve.wait_ge(selw_turned.sem, e + 1)
                        dve.tensor_copy(sel_wt, ps[:, 6, 0:S].rearrange("p (t n) -> p t n", t=NT)
                                        ).then_inc(selwt_ready.sem, 1)
                at = MOE_AT + 6 * ECH - 8
                chunk(at, r, e * ECH + (DCH + ECH), 1, tail=8)
                step = e * ECH + (DCH + ECH + 1)
                if not last_one:
                    take_gathered(e + 1)
                    for i in range(8, 14):
                        rest(at + i, r)
                    product(at + 11, r, step, 1)
                    rest(at + 14, r)
                for i in range(4):
                    t, n = divmod(i, 2)
                    dve.wait_ge(scattered.sem, e * 4 + (i + 1))
                    f = f_acc[:, t, n * 512:(n + 1) * 512]
                    dve.tensor_tensor(f, f, ps[:, 6 + n, :], ALU.add).then_inc(added.sem, 1)
                if not last_one:
                    rest_act(step, 1)
                    for i in range(15, 18):
                        rest(at + i, r)

            def take_gathered(e):
                banks = [ps[:, 6 + half, :].rearrange("p (k n) -> p k n", k=4) for half in range(2)]
                for half in range(2):
                    dve.wait_ge(gathered.sem, e * 2 + (half + 1))
                    dve.tensor_tensor(banks[half], banks[half], view(g_pre, 3 * KD + 4 * half, [[1, 4], [0, P]]), ALU.mult
                                      ).then_inc(hg_gained.sem, 1)
                for half in range(2):
                    dve.wait_ge(hghi_ready.sem, e * 2 + (half + 1))
                    dve.tensor_tensor(hg_lo[:, 4 * half:4 * half + 4, :], banks[half],
                                      hg_hi[:, 4 * half:4 * half + 4, :].bitcast(F32), ALU.subtract
                                      ).then_inc(hg_ready.sem, 1)

            def moe_pass(base):
                r, step = base * ECH, base * ECH + DCH + 1
                select(0)
                if base:
                    for i in range(3):
                        rest(MOE_AT + i, r)
                take_gathered(base)
                for i in (3, 4, 5):
                    rest(MOE_AT + i, r)
                product(MOE_AT + 3, r, step, 1)
                rest(MOE_AT + 6, r)
                rest_act(step, 1)
                for i in (7, 8, 9):
                    rest(MOE_AT + i, r)
                with dve.Fori(base, base + N_EXP - 1) as e:
                    expert(e, e - base if base else e, False)
                expert(base + N_EXP - 1, N_EXP - 1, True)

            setup()
            dve.wait_ge(con_landed.sem, 16)
            dve.wait_ge(gpre_landed.sem, 32)
            for layer in range(DEPTH):
                pre_norm(2 * layer, [(MIXER_AT[layer] + i, PIECE) for i in range(2)])
                mixer(layer)
                b0 = (DENSE_AT, MOE_AT)[layer]
                pre_norm(2 * layer + 1, [(b0 + 2, PIECE)])
                if layer % 2 == 0:
                    for i in (3, 4, 5):
                        rest(DENSE_AT + i, 0)
                    product(DENSE_AT + 3, 0, 1, NT)
                    rest(DENSE_AT + 6, 0)
                    rest_act(1, NT)
                    for i in (7, 8, 9):
                        rest(DENSE_AT + i, 0)
                    with dve.Fori(1, DCH - 1) as i:
                        chunk(DENSE_AT - 2, i, i + 1, NT)
                    chunk(DENSE_AT - 2, DCH - 1, DCH, NT, tail=8)
                    post_norm(1, lambda t: ps[:, 4 + 2 * t:6 + 2 * t, :])
            route()
            dve.memset(f_acc, 0.0).then_inc(f_zeroed.sem, 1)
            dve.wait_ge(f_zeroed.sem, 1)
            dve.wait_ge(over_ready.sem, 1)
            more = dve.value_load(over[0:1, 0:1])
            moe_pass(0)
            with dve.If(more > 0):
                dve.tensor_scalar(rt[:, 6, :], rt[:, 6, :], -float(P), None, ALU.add).then_inc(slots_shifted.sem, 1)
                dve.wait_ge(slots_shifted.sem, 1)
                moe_pass(N_EXP)
            dve.engine_nop().then_inc(f_summed.sem, 1)
            post_norm(3, lambda t: f_acc[:, t, :].rearrange("p (n c) -> p n c", n=2))


N_SMALL = NT + 3 + 1 + DEPTH + 2

_INS = ['x', 'positions', 'w_in', 'a_sinks', 'g_cq', 'w_uq', 'g_ckv', 'w_ukv', 'c_w1_k', 'c_w2_k', 'c_pe_k',
        'c_w1_v', 'c_w2_v', 'c_pe_v', 'g_oa', 'g_ob', 'g_oc', 'w_o', 'g_pre_mix', 'g_post_mix', 'g_pre_ffn',
        'g_post_ffn', 'ffn_w_gate', 'ffn_w_up', 'ffn_w_down', 'moe_router', 'moe_w_gate', 'moe_w_up', 'moe_w_down']


def kernel(**inputs):
    import concourse.bacc as _bacc
    from concourse.bass_utils import run_bass_kernel_spmd as _run

    nc = _bacc.Bacc("TRN2", target_bir_lowering=False, num_devices=1)
    arrays, aps = {}, {}

    def given(name, a):
        arrays[f"in_{name}_dram"] = a
        aps[name] = nc.dram_tensor(f"in_{name}_dram", a.shape, mybir.dt.from_np(a.dtype), kind="ExternalInput").ap()

    for name in _INS:
        given(name, np.ascontiguousarray(inputs[name]))
    given("consts", constants())
    out = nc.dram_tensor("out_0_dram", (1, S, D), F32, kind="ExternalOutput").ap()
    decoder_kernel(nc, aps["x"], aps["positions"], aps["consts"], aps, out)
    r = _run(nc, [arrays], core_ids=[0])
    return r.results[0]["out_0_dram"]
```

```python
from contextlib import ExitStack

import numpy as np

import concourse.bass as bass
from concourse import mybir

ALU = mybir.AluOpType
ACT = mybir.ActivationFunctionType
F32 = mybir.dt.float32
F32R = mybir.dt.float32r
I32 = mybir.dt.int32
AX_X = mybir.AxisListType.X

P = 128
D = 1024
S = 256
NT = S // P
DEPTH = 2
KD = D // P
EPS = 1e-6
HEAD = 64
A_HEADS, A_KV, A_WINDOW = 4, 2, 128
B_HEADS, B_QR, B_KVR, B_NOPE, B_ROPE = 4, 256, 128, 64, 32
C_HEADS, C_KV = 8, 2
CMP_BLOCK, CMP_STRIDE = 32, 16
N_CMP = (S - CMP_BLOCK) // CMP_STRIDE + 1
D_FF, D_FFE, N_EXP = 4096, 3584, 8
N_IN = 2232
QK_SCALE = HEAD ** -0.5
B_SCALE = (B_NOPE + B_ROPE) ** -0.5
MASKED = -1e30
TWO_PI = 2.0 * np.pi
PI_1 = 6.28125
PI_2 = float(np.float32(int((TWO_PI - PI_1) * 2 ** 20) / 2 ** 20))
PI_3 = float(TWO_PI - PI_1 - PI_2)
ROUND = 1.5 * 2 ** 23
SIN_MAX = 3.1415925
GELU_C = 2.0 * float(np.sqrt(2.0 / np.pi))

PIECE = 2048
RING = 6
SPLITS = 3
FCH = 512
ECH = D_FFE // FCH
DCH = D_FF // FCH
HALF_K = PIECE // FCH
HALF_F = PIECE // D
(LATENT_A, LATENT_B, CMP_IN, A_Q, A_KEYS, C_Q0, C_Q1, SW_KEYS, SW_VALUES) = range(9)
W_IN_COLS = ((512, 768), (768, 928), (1440, 1696), (0, 256), (256, 512), (928, 1184), (1184, 1440))
SW_COLS = (1696, 2208)
GATE_COLS = (2208, N_IN)
N_GATES = 3 * C_HEADS
W_IN_WIDTH = (256, 160 + N_GATES) + (256,) * 7
N_W_IN = len(W_IN_WIDTH)
N_MIXER = N_W_IN + KD // HALF_F
MIXER_AT = (0, N_MIXER + 6 * DCH)
DENSE_AT = N_MIXER
MOE_AT = MIXER_AT[1] + N_MIXER

A_SLOPES = [2.0 ** (-8.0 * (i + 1) / A_HEADS) for i in range(A_HEADS)]
C_SLOPES = [2.0 ** (-8.0 * (i + 1) / C_HEADS) for i in range(C_HEADS)]
JOBS = [("A", h) for h in range(A_HEADS)] + [("B", h) for h in range(B_HEADS)] \
    + [("S", h) for h in range(C_HEADS)] + [("W", h) for h in range(C_HEADS)]
NJ = len(JOBS)
SPAN = 3 * P

CONSTS = [("ident", P), ("tri", P), ("iota", P), ("dist_a", SPAN), ("dist_c", SPAN), ("mask_b", SPAN),
          ("dist_cmp", NT * N_CMP), ("inv_freq", B_ROPE // 2), ("has_cmp", NT)]
COL = {}
_at = 0
for _n, _w in CONSTS:
    COL[_n] = (_at, _w)
    _at += _w
N_CONST = _at


def constants():
    q = np.arange(P)[:, None]
    far = MASKED * 3.0
    span = np.concatenate([q - np.arange(P)[None], q + P - np.arange(2 * P)[None]], axis=1).astype(np.float32)
    cend = np.arange(N_CMP) * CMP_STRIDE + CMP_BLOCK - 1
    tok = np.arange(S).reshape(NT, P).T
    cmp_d = (tok[:, :, None] - cend[None, None]).astype(np.float32)
    t = {
        "ident": np.eye(P), "tri": np.triu(np.ones((P, P))),
        "iota": np.broadcast_to(np.arange(P), (P, P)),
        "dist_a": np.where((span >= 0) & (span < A_WINDOW), -span, far),
        "dist_c": np.where(span >= 0, -span, far),
        "mask_b": np.where(span >= 0, 0.0, MASKED),
        "dist_cmp": np.where(cmp_d >= 0, -cmp_d, far).reshape(P, -1),
        "inv_freq": np.broadcast_to(10000.0 ** (-np.arange(0, B_ROPE, 2, dtype=np.float32) / B_ROPE), (P, B_ROPE // 2)),
        "has_cmp": (tok >= CMP_BLOCK - 1),
    }
    return np.ascontiguousarray(np.concatenate([np.asarray(t[n], np.float32) for n, _ in CONSTS], axis=1))


class Stage:

    def __init__(self, sem, per_round):
        self.sem, self.per_round = sem, per_round

    def at(self, rnd, k):
        return rnd * self.per_round + k


def decoder_kernel(nc, x_in, pos_in, consts_in, w, out):
    with ExitStack() as ctx:
        def sb(name, shape, dt=F32):
            return ctx.enter_context(nc.sbuf_tensor(name, shape, dt))

        def stage(name, per_round):
            return Stage(ctx.enter_context(nc.semaphore(name)), per_round)

        ps = ctx.enter_context(nc.psum_tensor("ps", [P, 8, 512], F32))

        def view(t, off, dims, p0=0, np_=P):
            pitch = 1
            for n in t.shape[1:]:
                pitch *= n
            return bass.AP(t, p0 * pitch + off, [[pitch, np_]] + [list(d) for d in dims])

        zone_at = -(-nc.sbuf_base // 32) * 32
        zone = sb("zone", [P, 16384])

        def split_view(name, off, dims):
            return nc.alloc_sbuf_tensor_at(name, [P] + dims, F32R, offset=zone_at + 4 * off)

        raw = sb("raw", [P, RING, PIECE])
        w_hi = sb("w_hi", [P, SPLITS, PIECE], F32R)
        w_lo = sb("w_lo", [P, SPLITS, PIECE], F32R)
        w1 = sb("w1", [P, 2, 16 * P])
        x = sb("x", [P, NT, D])
        con = sb("con", [P, N_CONST])
        w_uq = sb("w_uq", [P, 2, 384])
        w_ukv = sb("w_ukv", [P, 512])
        w2 = sb("w2", [P, 2, HEAD])
        pe_raw = sb("pe_raw", [16, 2, P])
        pe_t = sb("pe_t", [P, 2, 16])
        router = sb("router", [P, KD, N_EXP])
        g_post = sb("g_post", [P, D])
        g_in = sb("g_in", [P, D])
        g_cq = sb("g_cq", [P, DEPTH, 2])
        g_ckv = sb("g_ckv", [P, DEPTH])
        sinks = sb("sinks", [P, DEPTH, A_HEADS])
        neg_sinks = sb("neg_sinks", [P, DEPTH, A_HEADS])
        pos_i = sb("pos_i", [P, NT], I32)
        pos_f = sb("pos_f", [P, NT])
        sincos = sb("sincos", [P, 2, NT, 16])
        kc_t = sb("kc_t", [P, 16])
        mean = sb("mean", [P, 8])
        rstd = sb("rstd", [P, 8])
        var = sb("var", [P, 8])
        minus_half = sb("minus_half", [P, 8])
        nmax = sb("nmax", [P, NJ, 2])
        rsum = sb("rsum", [P, NJ, 2])
        rinv = sb("rinv", [P, NJ, 2])
        sink_e = sb("sink_e", [P, A_HEADS, 2])
        gate = sb("gate", [P, NT, 3 * C_HEADS])
        gscale = sb("gscale", [P, NT, C_HEADS])
        cmax = sb("cmax", [P, 16])
        csum = sb("csum", [P, 16])
        rt = sb("rt", [P, 12, 16])
        cnt = sb("cnt", [P, 4])
        over = sb("over", [P, 1], I32)

        def c(name):
            a, n = COL[name]
            return con[:, a:a + n]

        def zv(off, *dims):
            n = 1
            for d in dims:
                n *= d
            v = zone[:, off:off + n]
            if len(dims) == 2:
                v = v.rearrange("p (a b) -> p a b", b=dims[1])
            if len(dims) == 3:
                v = v.rearrange("p (a b c) -> p a b c", b=dims[1], c=dims[2])
            return v

        HN, HT, FO = 0, 2048, 4096
        hn = zv(HN, NT, D)
        h_hi = split_view("h_hi", HT, [KD, S])
        h_lo = split_view("h_lo", FO, [KD, S])
        f_acc = zv(FO, NT, D)
        o_all = f_acc
        blk = zv(HN, 2, 480)
        c_tmp = zv(HN, 512)
        pt = zv(HN + 1024, 2, SPAN)
        sc_sb = zv(HT, 5, SPAN)
        pt_cmp = zv(HN + 512, 4, P)
        Z = 6144
        XS_AT = Z + 3072
        aq_t = zv(Z, 2, S)
        akv = zv(Z + 512, 512)
        cq_t = zv(Z + 1024, 4, S)
        mix_hi = [split_view("mix_hi_ab", XS_AT, [4, S]), split_view("mix_hi_c", Z, [4, S])]
        mix_lo = [split_view("mix_lo_ab", XS_AT + 1024, [4, S]), split_view("mix_lo_c", Z + 1024, [4, S])]
        KS, KW, XS, BL = Z + 2048, Z + 2560, Z + 3072, Z + 4096
        ksv = zv(KS, 512)
        kwv = zv(KW, 512)
        bl = zv(BL, NT, 416)
        CQN = BL + 832
        cqn_t = zv(CQN, 3, S)
        qn = zv(CQN + 768, NT, 256)
        o_t = zv(CQN + 768, 2, S)
        kvb = zv(CQN + 1280, NT, 512)
        ROPE_IN = CQN + 2304
        ROPE_A, ROPE_B, ROPE_O = ROPE_IN + 320, ROPE_IN + 640, ROPE_IN + 960
        p_cmp = zv(ROPE_IN, 16, 32)
        hid = zv(ROPE_IN + 512, 4, 64)
        QN_T = ROPE_O + 512
        qn_t = zv(QN_T, 2, S)
        kn_t = zv(QN_T + 512, 2, S)
        qkr_t = zv(QN_T + 1024, 2, S)
        assert QN_T + 1536 <= 16384
        ang = zv(QN_T, 2 * NT, 16)
        turns = zv(QN_T + 64, 2 * NT, 16)
        v_cmp = zv(CQN, C_KV, 256)
        hg_hi = split_view("hg_hi", 6144, [KD, P])
        hg_lo = split_view("hg_lo", 7168, [KD, P])
        act_hi = split_view("act_hi", 8192, [NT, FCH])
        act_lo = split_view("act_lo", 9216, [NT, FCH])
        sil = zv(10240, NT, FCH)
        y_sb = zv(11264, 2, 512)
        sel = zv(12288, NT, P)
        sel_w = zv(12544, NT, P)
        sel_wt = zv(12800, NT, P)
        ones = zv(13056, P)

        x_landed = stage("x_landed", 0)
        con_landed = stage("con_landed", 0)
        gin_landed = stage("gin_landed", 80)
        gates_landed = stage("gates_landed", 16)
        small_landed = stage("small_landed", 0)
        aux_landed = stage("aux_landed", 16 * 6)
        gpost_landed = stage("gpost_landed", 16)
        slot_landed = [stage(f"slot_landed{i}", 0) for i in range(RING)]
        w1_landed = stage("w1_landed", 32)
        hi_ready = stage("hi_ready", 0)
        lo_ready = stage("lo_ready", 0)
        piece_used = stage("piece_used", 0)
        out_stored = stage("out_stored", 0)
        sin_ready = stage("sin_ready", 0)
        sin_done = stage("sin_done", 0)
        pre_sq = stage("pre_sq", NT)
        pre_rstd = stage("pre_rstd", NT)
        post_rstd = stage("post_rstd", NT)
        lat_rstd = stage("lat_rstd", 1)
        o_rstd = stage("o_rstd", 2)
        pool_chain = stage("pool_chain", 0)
        hn_ready = stage("hn_ready", NT)
        hn_turned = stage("hn_turned", 4)
        hhi_ready = stage("hhi_ready", 4)
        h_ready = stage("h_ready", 4)
        post_sq = stage("post_sq", NT)
        x_updated = stage("x_updated", NT)
        proj_out_a = stage("proj_out_a", 6)
        proj_out_d = stage("proj_out_d", 6)
        lat_sq = stage("lat_sq", 4)
        lat_ready = stage("lat_ready", 1)
        lat_turned = stage("lat_turned", 2)
        latt_ready = stage("latt_ready", 2)
        latup_done = stage("latup_done", 4)
        latup_out = stage("latup_out", 2)
        kv_out = stage("kv_out", 2)
        qk_ready = stage("qk_ready", 1)
        qk_turned = stage("qk_turned", 3)
        qk_out = stage("qk_out", 3)
        pe_turned = stage("pe_turned", 1)
        blk_ready = stage("blk_ready", 2)
        hid_done = stage("hid_done", 2)
        gelu_arg = stage("gelu_arg", 1)
        gelu_exp = stage("gelu_exp", 1)
        gates_exp = stage("gates_exp", 1)
        gelu_ready = stage("gelu_ready", 1)
        ckv_done = stage("ckv_done", 2)
        ckv_out = stage("ckv_out", 1)
        cs_done = stage("cs_done", 1)
        cs_arg = stage("cs_arg", 1)
        cs_exp = stage("cs_exp", 1)
        cp_turned = stage("cp_turned", 1)
        cp_out = stage("cp_out", 1)
        co_done = stage("co_done", 1)
        co_out = stage("co_out", 1)
        score_done = stage("score_done", NJ)
        biased = stage("biased", NJ)
        max_ready = stage("max_ready", NJ)
        probs_ready = stage("probs_ready", NJ)
        probs_turned = stage("probs_turned", NJ)
        pt_ready = stage("pt_ready", NJ)
        pv_done = stage("pv_done", NJ)
        ot_ready = stage("ot_ready", NJ // 2)
        turned_back = stage("turned_back", NJ // 2)
        sink_arg = stage("sink_arg", 1)
        sink_exp = stage("sink_exp", 1)
        o_out = stage("o_out", 4)
        o_sq = stage("o_sq", 6)
        mixed_ready = stage("mixed_ready", 2)
        mixed_turned = stage("mixed_turned", 4)
        mixhi_ready = stage("mixhi_ready", 4)
        mix_ready = stage("mix_ready", 4)
        silu_ready = stage("silu_ready", 0)
        prod_ready = stage("prod_ready", 0)
        act_turned = stage("act_turned", 0)
        acthi_ready = stage("acthi_ready", 0)
        act_ready = stage("act_ready", 0)
        logit_done = stage("logit_done", 0)
        route_arg = stage("route_arg", 0)
        route_exp = stage("route_exp", 0)
        picks_ready = stage("picks_ready", 0)
        ranks_done = stage("ranks_done", 0)
        over_ready = stage("over_ready", 0)
        f_zeroed = stage("f_zeroed", 0)
        slots_shifted = stage("slots_shifted", 0)
        f_summed = stage("f_summed", 0)
        sel_ready = stage("sel_ready", 0)
        gathered = stage("gathered", 0)
        hghi_ready = stage("hghi_ready", 0)
        hg_ready = stage("hg_ready", 0)
        selw_ready = stage("selw_ready", 0)
        selw_turned = stage("selw_turned", 0)
        selwt_ready = stage("selwt_ready", 0)
        y_ready = stage("y_ready", 0)
        scattered = stage("scattered", 0)
        added = stage("added", 0)
        dve_chain = stage("dve_chain", 0)

        def wait_piece(eng, stage_, n, r):
            eng.wait_ge(stage_.sem, r * RING + (n + 1))

        LAT_KV_BANKS = (7, 2)
        block = ctx.enter_context(nc.Block())

        @block.sync
        def _(sp):
            def load(n, r, src, k, pitch=None):
                if n >= RING or not isinstance(r, int):
                    wait_piece(sp, lo_ready, n - RING, r)
                cols = [[1, src.shape[-1]]] if len(src.shape) == 3 else [[src.shape[-1], src.shape[-2]], [1, src.shape[-1]]]
                width = pitch or int(np.prod(src.shape[2:]))
                sp.dma_start(view(raw, n % RING * PIECE, [[width, k]] + cols), src
                             ).then_inc(slot_landed[n % RING].sem, 16)

            def w_in_piece(layer, i):
                rows = w["w_in"][layer].rearrange("(p k) n -> p k n", k=KD)
                n = MIXER_AT[layer] + i
                if i >= SW_KEYS:
                    src = rows[:, :, SW_COLS[0]:SW_COLS[1]].rearrange("p k (b i n) -> p k b i n", b=2, i=2)
                    load(n, 0, src[:, :, :, i - SW_KEYS, :], KD)
                    return
                if i == LATENT_B:
                    if n >= RING:
                        wait_piece(sp, lo_ready, n - RING, 0)
                    sp.dma_start(view(raw, n % RING * PIECE + 160, [[W_IN_WIDTH[i], KD], [1, N_GATES]]),
                                 rows[:, :, GATE_COLS[0]:GATE_COLS[1]]).then_inc(gates_landed.sem, 16)
                a, b = W_IN_COLS[i]
                load(n, 0, rows[:, :, a:b], KD, W_IN_WIDTH[i])

            def w_o_piece(layer, i):
                load(MIXER_AT[layer] + N_W_IN + i, 0, w["w_o"][layer].rearrange("(k p) n -> p k n", p=P)
                     [:, HALF_F * i:HALF_F * (i + 1), :], HALF_F)

            def up_pieces(n, r, wt, ch):
                for half in range(2):
                    load(n + half, r, wt.rearrange("(p k) (c n) -> c p k n", k=KD, n=FCH)[ch]
                         [:, HALF_K * half:HALF_K * (half + 1), :], HALF_K)

            def down_pieces(n, r, wt, ch):
                for half in range(2):
                    load(n + half, r, wt.rearrange("(c f p) n -> c p f n", p=P, f=FCH // P)[ch]
                         [:, HALF_F * half:HALF_F * (half + 1), :], HALF_F)

            def w1_load(layer):
                if layer:
                    sp.wait_ge(hid_done.sem, hid_done.at(layer - 1, 2))
                for i, name in enumerate(("c_w1_k", "c_w1_v")):
                    sp.dma_start(w1[:, i, :].rearrange("p (a e) -> p a e", e=P),
                                 w[name][layer].rearrange("(a b) d e -> (b d) a e", b=2)).then_inc(w1_landed.sem, 16)

            def aux_loads(layer):
                if layer:
                    sp.wait_ge(ckv_done.sem, ckv_done.at(layer - 1, 2))
                    sp.wait_ge(latup_done.sem, latup_done.at(layer - 1, 4))
                for dst, src in (
                    (w_uq[:, :, :], w["w_uq"][layer].rearrange("(p k) n -> p k n", k=2)),
                    (w_ukv[:, :], w["w_ukv"][layer]),
                    (w2[:, 0, :], w["c_w2_k"][layer]),
                    (w2[:, 1, :], w["c_w2_v"][layer]),
                    (pe_raw[:, 0, :], w["c_pe_k"][layer].rearrange("(a b) d -> a (b d)", b=2)),
                    (pe_raw[:, 1, :], w["c_pe_v"][layer].rearrange("(a b) d -> a (b d)", b=2)),
                ):
                    sp.dma_start(dst, src).then_inc(aux_landed.sem, 16)

            def gpost_load(b):
                name = ("g_post_mix", "g_post_ffn")[b % 2]
                if b:
                    sp.wait_ge(x_updated.sem, x_updated.at(b - 1, NT))
                sp.dma_start(g_post[:, :], bass.AP(w[name].tensor, (b // 2) * D, [[0, P], [1, D]])
                             ).then_inc(gpost_landed.sem, 16)

            def gin_load(src, a, n, at):
                sp.dma_start(g_in[:, a:a + n], bass.AP(w[src].tensor, at, [[0, P], [1, n]])
                             ).then_inc(gin_landed.sem, 16)

            def gpre_load(b):
                if b % 2:
                    sp.wait_ge(mixed_ready.sem, mixed_ready.at(b // 2, 2))
                elif b:
                    sp.wait_ge(hn_ready.sem, hn_ready.at(b - 1, NT))
                gin_load(("g_pre_mix", "g_pre_ffn")[b % 2], 0, D, b // 2 * D)

            def gmix_load(layer):
                sp.wait_ge(hn_ready.sem, hn_ready.at(2 * layer, NT))
                gin_load("g_oa", 0, 256, layer * 256)
                gin_load("g_ob", 256, 256, layer * 256)
                gin_load("g_oc", 512, 512, layer * 512)

            for t in range(NT):
                sp.dma_start(x[:, t, :], x_in[0, t * P:(t + 1) * P, :]).then_inc(x_landed.sem, 16)
            gpre_load(0)
            sp.wait_ge(con_landed.sem, 16)
            sp.wait_ge(gin_landed.sem, 16)
            for i in range(RING):
                w_in_piece(0, i)
            aux_loads(0)
            w1_load(0)
            gpost_load(0)
            gmix_load(0)
            for i in range(RING, N_W_IN):
                w_in_piece(0, i)
            for i in range(KD // HALF_F):
                w_o_piece(0, i)
            dg, du, dd = w["ffn_w_gate"][0], w["ffn_w_up"][0], w["ffn_w_down"][0]
            up_pieces(DENSE_AT, 0, dg, 0)
            w1_load(1)
            aux_loads(1)
            up_pieces(DENSE_AT + 2, 0, du, 0)
            up_pieces(DENSE_AT + 4, 0, dg, 1)
            gpre_load(1)
            gpost_load(1)
            gpre_load(2)
            with sp.Fori(1, DCH - 1) as i:
                up_pieces(DENSE_AT, i, du, i)
                down_pieces(DENSE_AT + 2, i, dd, i - 1)
                up_pieces(DENSE_AT + 4, i, dg, i + 1)
            up_pieces(DENSE_AT, DCH - 1, du, DCH - 1)
            down_pieces(DENSE_AT + 2, DCH - 1, dd, DCH - 2)
            down_pieces(DENSE_AT + 4, DCH - 1, dd, DCH - 1)
            for i in range(N_W_IN):
                w_in_piece(1, i)
                if i == RING:
                    gpost_load(2)
                    gmix_load(1)
            for i in range(KD // HALF_F):
                w_o_piece(1, i)

            def expert_pieces(r, ei, gains=False):
                mg, mu, md = w["moe_w_gate"][0][ei], w["moe_w_up"][0][ei], w["moe_w_down"][0][ei]
                for ch in range(ECH + 1):
                    at = MOE_AT + 6 * ch - 2
                    if ch == 0:
                        up_pieces(MOE_AT, r, mg, 0)
                        up_pieces(MOE_AT + 2, r, mu, 0)
                    elif ch < ECH:
                        up_pieces(at, r, mg, ch)
                        if gains and ch == 1:
                            gpre_load(3)
                            gpost_load(3)
                        up_pieces(at + 2, r, mu, ch)
                        down_pieces(at + 4, r, md, ch - 1)
                    else:
                        down_pieces(at, r, md, ch - 1)

            expert_pieces(0, 0, gains=True)
            with sp.Fori(1, N_EXP) as e:
                expert_pieces(e * ECH, e)
            sp.wait_ge(over_ready.sem, 1)
            more = sp.value_load(over[0:1, 0:1])
            with sp.If(more > 0):
                with sp.Fori(N_EXP, 2 * N_EXP) as e:
                    expert_pieces(e * ECH, e - N_EXP)
            for t in range(NT):
                sp.wait_ge(x_updated.sem, x_updated.at(3, t + 1))
                sp.dma_start(out[0, t * P:(t + 1) * P, :], x[:, t, :]).then_inc(out_stored.sem, 16)
            sp.wait_ge(out_stored.sem, 16 * NT)

        @block.gpsimd
        def _(pool):
            chain = [0]

            def to_rstd(a, n, stage_in, count, stage_out):
                pool.wait_ge(stage_in.sem, count)
                chain[0] += 1
                pool.tensor_scalar(var[:, a:a + n], mean[:, a:a + n], EPS, None, ALU.add).then_inc(pool_chain.sem, 1)
                pool.wait_ge(pool_chain.sem, chain[0])
                pool.tensor_tensor(rstd[:, a:a + n], var[:, a:a + n], minus_half[:, a:a + n], ALU.pow
                                   ).then_inc(stage_out.sem, 1)

            chain[0] += 1
            pool.memset(minus_half[:, :], -0.5).then_inc(pool_chain.sem, 1)
            pool.wait_ge(pool_chain.sem, 1)
            for layer in range(DEPTH):
                for half in range(2):
                    b = 2 * layer + half
                    for t in range(NT):
                        to_rstd(t, 1, pre_sq, pre_sq.at(b, t + 1), pre_rstd)
                    if half == 0:
                        to_rstd(0, 4, lat_sq, lat_sq.at(layer, 4), lat_rstd)
                        to_rstd(0, 4, o_sq, o_sq.at(layer, 4), o_rstd)
                        to_rstd(4, 2, o_sq, o_sq.at(layer, 6), o_rstd)
                    for t in range(NT):
                        to_rstd(t, 1, post_sq, post_sq.at(b, t + 1), post_rstd)

        @block.tensor
        def _(pe):
            ident = c("ident")

            def passes(out, lhs, rhs, start, stop):
                pe.matmul(out, lhs[0], rhs[0], start=start, stop=False, skip_group_check=True)
                pe.matmul(out, lhs[0], rhs[1], start=False, stop=False, skip_group_check=True)
                return pe.matmul(out, lhs[1], rhs[0], start=False, stop=stop, skip_group_check=True)

            def piece_view(n, off, dims):
                at = n % SPLITS * PIECE + off
                return view(w_hi, at, dims), view(w_lo, at, dims)

            def turn_h(b):
                for t in range(NT):
                    pe.wait_ge(hn_ready.sem, hn_ready.at(b, t + 1))
                    for half in range(2):
                        for k in range(4):
                            last = pe.transpose(ps[:, 2 * t + half, k * P:(k + 1) * P],
                                                view(zone, HN + t * D + 4 * half + k, [[KD, P]]), ident)
                        last.then_inc(hn_turned.sem, 1)

            def project(layer):
                def begin(i):
                    wait_piece(pe, lo_ready, MIXER_AT[layer] + i, 0)

                def end(last):
                    last.then_inc(piece_used.sem, 1)

                def wcols(i, k, a, n):
                    return piece_view(MIXER_AT[layer] + i, k * W_IN_WIDTH[i] + a, [[1, n]])

                def feature_major(bank, col, i, a):
                    for k in range(KD):
                        last = passes(ps[:, bank, col:col + S], wcols(i, k, a, P), (h_hi[:, k, :], h_lo[:, k, :]),
                                      k == 0, k == KD - 1)
                    return last

                def token_major(bank, col, i, a, n, t):
                    for k in range(KD):
                        last = passes(ps[:, bank, col:col + n],
                                      (h_hi[:, k, t * P:(t + 1) * P], h_lo[:, k, t * P:(t + 1) * P]),
                                      wcols(i, k, a, n), k == 0, k == KD - 1)
                    return last

                pe.wait_ge(h_ready.sem, h_ready.at(2 * layer, 4))
                for i, col, n in ((LATENT_A, 0, 256), (LATENT_B, 256, 160 + N_GATES)):
                    begin(i)
                    for t in range(NT):
                        last = token_major(2 + t, col, i, 0, n, t)
                    end(last)
                for i, bank in ((CMP_IN, 6), (A_Q, 0)):
                    begin(i)
                    for j in range(2):
                        last = feature_major(bank, j * S, i, j * P)
                    end(last)
                pe.wait_ge(aux_landed.sem, aux_landed.at(layer + 1, 0))
                for i in range(2):
                    last = pe.transpose(ps[:, 7, i * 16:(i + 1) * 16], pe_raw[:, i, :], ident[0:16, 0:16])
                last.then_inc(pe_turned.sem, 1)
                pe.wait_ge(lat_ready.sem, lat_ready.at(layer, 1))
                for k in range(2):
                    for t in range(NT):
                        last = pe.transpose(ps[:, 3, k * S + t * P:k * S + (t + 1) * P],
                                            view(zone, BL + t * 416 + k, [[2, P]]), ident)
                last.then_inc(lat_turned.sem, 1)
                for t in range(NT):
                    last = pe.transpose(ps[:, 2, t * P:(t + 1) * P], bl[:, t, 256:384], ident)
                last.then_inc(lat_turned.sem, 1)
                begin(A_KEYS)
                feature_major(1, 0, A_KEYS, 0)
                for t in range(NT):
                    last = token_major(1, S + t * P, A_KEYS, P, P, t)
                end(last)
                pe.wait_ge(latt_ready.sem, latt_ready.at(layer, 2))
                for t in range(NT):
                    for k in range(2):
                        last = pe.matmul(ps[:, 4 + t, 0:384], cqn_t[:, k, t * P:(t + 1) * P], w_uq[:, k, :],
                                         start=(k == 0), stop=(k == 1))
                    last.then_inc(latup_done.sem, 1)
                for t in range(NT):
                    pe.matmul(ps[:, LAT_KV_BANKS[t], :], cqn_t[:, 2, t * P:(t + 1) * P], w_ukv[:, :],
                              start=True, stop=True).then_inc(latup_done.sem, 1)
                pe.wait_ge(w1_landed.sem, w1_landed.at(layer, 32))
                for i in range(2):
                    pe.wait_ge(blk_ready.sem, blk_ready.at(layer, i + 1))
                    for a in range(16):
                        last = pe.matmul(ps[:, 6, 32 * i:32 * i + 30],
                                         w1[:, i, a * P:(a + 1) * P],
                                         blk[:, i, a * 30:(a + 1) * 30], start=(a == 0), stop=(a == 15))
                    last.then_inc(hid_done.sem, 1)
                for g in range(2):
                    begin(C_Q0 + g)
                    pe.wait_ge(latup_out.sem, latup_out.at(layer, g + 1))
                    for j in range(2):
                        last = feature_major(4 + g, j * S, C_Q0 + g, j * P)
                    end(last)
                pe.wait_ge(qk_ready.sem, qk_ready.at(layer, 1))
                for pair in range(2):
                    for t in range(NT):
                        last = pe.transpose(ps[:, 3, pair * S + t * P:pair * S + (t + 1) * P],
                                            qn[:, t, pair * P:(pair + 1) * P], ident)
                last.then_inc(qk_turned.sem, 1)
                pe.wait_ge(kv_out.sem, kv_out.at(layer, 2))
                for pair in range(2):
                    for t in range(NT):
                        last = pe.transpose(ps[:, 2, pair * S + t * P:pair * S + (t + 1) * P],
                                            kvb[:, t, pair * P:(pair + 1) * P], ident)
                last.then_inc(qk_turned.sem, 1)
                for i in range(2):
                    for t in range(NT):
                        last = pe.transpose(ps[:, 7, i * S + t * P:i * S + (t + 1) * P],
                                            zone[:, ROPE_O + i * S + t * P:ROPE_O + i * S + (t + 1) * P], ident)
                last.then_inc(qk_turned.sem, 1)
                pe.wait_ge(gelu_ready.sem, gelu_ready.at(layer, 1))
                for g in range(2):
                    last = pe.matmul(ps[64 * g:64 * g + 64, 6, 64:64 + N_CMP], w2[:, 0, :],
                                     hid[:, 0, g * 15:g * 15 + 15], start=True, stop=True)
                last.then_inc(ckv_done.sem, 1)
                for i in range(4):
                    for g in range(2):
                        last = pe.matmul(ps[32 * i:32 * i + N_CMP, 6, 128 + g * HEAD:128 + (g + 1) * HEAD],
                                         hid[:, 0, 32 + g * 15:32 + g * 15 + 15], w2[:, 1, :], start=True, stop=True)
                last.then_inc(ckv_done.sem, 1)
                begin(SW_KEYS)
                pe.wait_ge(proj_out_a.sem, proj_out_a.at(layer, 3))
                for j in range(2):
                    last = feature_major(0, j * S, SW_KEYS, j * P)
                end(last)
                pe.wait_ge(ckv_out.sem, ckv_out.at(layer, 1))
                pe.wait_ge(qk_out.sem, qk_out.at(layer, 3))
                pe.wait_ge(proj_out_a.sem, proj_out_a.at(layer, 5))
                pe.wait_ge(proj_out_d.sem, proj_out_d.at(layer, 5))
                for t in range(NT):
                    for h in range(C_HEADS):
                        g, j = divmod(h, 4)
                        last = pe.matmul(ps[:, 6 + g, (t * 4 + j) * 16:(t * 4 + j) * 16 + N_CMP],
                                         cq_t[64 * g:64 * g + 64, j, t * P:(t + 1) * P],
                                         kc_t[64 * g:64 * g + 64, 0:N_CMP], start=True, stop=True)
                last.then_inc(cs_done.sem, 1)
                begin(SW_VALUES)
                for t in range(NT):
                    last = token_major(1, t * 256, SW_VALUES, 0, 256, t)
                end(last)
                pe.wait_ge(proj_out_a.sem, proj_out_a.at(layer, 6))
                pe.wait_ge(proj_out_d.sem, proj_out_d.at(layer, 6))

            def operands(kind, h):
                if kind == "B":
                    half, pair = h % 2, h // 2
                    n, r = slice(64 * half, 64 * half + 64), slice(32 * h, 32 * h + 32)
                    return ([(qn_t[n, pair, :], kn_t[n, pair, :]), (qkr_t[r, 0, :], qkr_t[r, 1, :])],
                            lambda t: kvb[:, t, 256 + h * HEAD:256 + (h + 1) * HEAD])
                g, j = divmod(h, 2 if kind == "A" else 4)
                q = aq_t if kind == "A" else cq_t
                kv = {"A": akv, "S": ksv, "W": kwv}[kind]
                n = slice(64 * g, 64 * g + 64)
                return ([(q[n, j, :], kv[n, 0:S])],
                        lambda t: kv[:, S + t * P + g * HEAD:S + t * P + (g + 1) * HEAD])

            def attention(layer):
                pe.wait_ge(cs_exp.sem, cs_exp.at(layer, 1))
                for t in range(NT):
                    for g in range(2):
                        last = pe.transpose(ps[:, 2, (2 * t + g) * P:(2 * t + g + 1) * P],
                                            view(zone, ROPE_IN + (t * 8 + 4 * g) * 32, [[1, P]]), ident)
                last.then_inc(cp_turned.sem, 1)

                def scores(j):
                    kind, h = JOBS[j]
                    if j >= 2:
                        pe.wait_ge(biased.sem, biased.at(layer, j - 1))
                    pairs, _ = operands(kind, h)
                    for dst, q0, n in ((ps[:, j % 2, 0:P], 0, P), (ps[:, j % 2, P:SPAN], P, S)):
                        for i, (q, k) in enumerate(pairs):
                            last = pe.matmul(dst, q[:, q0:q0 + P], k[:, 0:n], start=(i == 0), stop=(i == len(pairs) - 1))
                    last.then_inc(score_done.sem, 1)

                def turn(j):
                    pe.wait_ge(probs_ready.sem, probs_ready.at(layer, j + 1))
                    if j == 0:
                        pe.wait_ge(cp_out.sem, cp_out.at(layer, 1))
                    elif j >= 2:
                        pe.wait_ge(pt_ready.sem, pt_ready.at(layer, j - 1))
                    for b in range(3):
                        last = pe.transpose(ps[:, 2 + j % 2, b * P:(b + 1) * P], sc_sb[:, j % 5, b * P:(b + 1) * P], ident)
                    last.then_inc(probs_turned.sem, 1)

                def values(j):
                    kind, h = JOBS[j]
                    pe.wait_ge(pt_ready.sem, pt_ready.at(layer, j + 1))
                    if j >= 4 and j % 2 == 0:
                        pe.wait_ge(ot_ready.sem, ot_ready.at(layer, j // 2 - 1))
                    _, v = operands(kind, h)
                    rows, bank = slice(64 * (j % 2), 64 * (j % 2) + 64), 4 + j // 2 % 2
                    pe.matmul(ps[rows, bank, 0:S], v(0), pt[:, j % 2, 0:2 * P], start=True, stop=False,
                              skip_group_check=True)
                    pe.matmul(ps[rows, bank, P:S], v(1), pt[:, j % 2, 2 * P:SPAN], start=False, stop=True,
                              skip_group_check=True).then_inc(pv_done.sem, 1)

                def turn_back(p):
                    if p == 0:
                        pe.wait_ge(co_out.sem, co_out.at(layer, 1))
                    elif p % 4 == 0:
                        pe.wait_ge(o_out.sem, o_out.at(layer, 1 + p // 4))
                    pe.wait_ge(ot_ready.sem, ot_ready.at(layer, p + 1))
                    for t in range(NT):
                        last = pe.transpose(ps[:, 6 + t, (p % 4) * P:(p % 4 + 1) * P], o_t[:, p % 2, t * P:(t + 1) * P],
                                            ident)
                    last.then_inc(turned_back.sem, 1)

                for j in range(NJ + 6):
                    if j < NJ:
                        scores(j)
                    if j == 1:
                        pe.wait_ge(cp_out.sem, cp_out.at(layer, 1))
                        for t in range(NT):
                            for g in range(2):
                                last = pe.matmul(ps[:, 6 + t, g * 256:(g + 1) * 256], pt_cmp[:, 2 * t + g, :],
                                                 v_cmp[:, g, :], start=True, stop=True)
                        last.then_inc(co_done.sem, 1)
                    if 0 <= j - 3 < NJ:
                        turn(j - 3)
                    if 0 <= j - 4 < NJ:
                        values(j - 4)
                    if j >= 7 and j % 2 == 1:
                        turn_back((j - 7) // 2)
                    if j == 25:
                        pe.wait_ge(biased.sem, biased.at(layer, NJ))
                        turn_mixed(layer, 0)

            def turn_mixed(layer, part):
                pe.wait_ge(mixed_ready.sem, mixed_ready.at(layer, part + 1))
                for t in range(NT):
                    for k in range(4):
                        a = part * 512 + k * P
                        last = pe.transpose(ps[:, 6 * part + t, k * P:(k + 1) * P], o_all[:, t, a:a + P], ident)
                    last.then_inc(mixed_turned.sem, 1)

            def output_projection(layer):
                pe.wait_ge(mix_ready.sem, mix_ready.at(layer, 2))
                for i in range(KD // HALF_F):
                    n = MIXER_AT[layer] + N_W_IN + i
                    part = i // 2
                    if i == 1:
                        turn_mixed(layer, 1)
                    if i == 2:
                        pe.wait_ge(mix_ready.sem, mix_ready.at(layer, 4))
                    wait_piece(pe, lo_ready, n, 0)
                    for kk in range(HALF_F):
                        k = HALF_F * i + kk
                        for t in range(NT):
                            lhs = [m[part][:, k % 4, t * P:(t + 1) * P] for m in (mix_hi, mix_lo)]
                            for half in range(2):
                                last = passes(ps[:, 2 * t + half, :], lhs,
                                              piece_view(n, kk * D + half * 512, [[1, 512]]), k == 0, k == KD - 1)
                    last.then_inc(piece_used.sem, 1)

            def hidden(n, r, bank, lhs, tiles):
                for half in range(2):
                    wait_piece(pe, lo_ready, n + half, r)
                    for t in range(tiles):
                        for kk in range(HALF_K):
                            k = HALF_K * half + kk
                            last = passes(ps[:, bank + t, :], lhs(k, t),
                                          piece_view(n + half, kk * FCH, [[1, FCH]]), k == 0, k == KD - 1)
                    last.then_inc(piece_used.sem, 1)

            def gate_up(n, r, step, lhs, tiles, first=False):
                if not first:
                    pe.wait_ge(silu_ready.sem, step - 1)
                hidden(n, r, 0, lhs, tiles)
                if not first:
                    pe.wait_ge(act_ready.sem, step - 1)
                hidden(n + 2, r, 2, lhs, tiles)

            def turn(step, tiles):
                pe.wait_ge(prod_ready.sem, step)
                for t in range(tiles):
                    for f in range(FCH // P):
                        last = pe.transpose(ps[:, 2 + t, f * P:(f + 1) * P], sil[:, t, f * P:(f + 1) * P], ident)
                last.then_inc(act_turned.sem, 1)

            def down(n, r, step, tiles, first, last_one):
                pe.wait_ge(act_ready.sem, step)
                for half in range(2):
                    wait_piece(pe, lo_ready, n + half, r)
                    for ff in range(HALF_F):
                        f = HALF_F * half + ff
                        for t in range(tiles):
                            lhs = act_hi[:, t, f * P:(f + 1) * P], act_lo[:, t, f * P:(f + 1) * P]
                            for c2 in range(2):
                                last = passes(ps[:, 4 + 2 * t + c2, :], lhs,
                                              piece_view(n + half, ff * D + c2 * 512, [[1, 512]]),
                                              first and f == 0, last_one and f == FCH // P - 1)
                    last.then_inc(piece_used.sem, 1)

            def dense():
                def tokens(k, t):
                    return h_hi[:, k, t * P:(t + 1) * P], h_lo[:, k, t * P:(t + 1) * P]

                pe.wait_ge(h_ready.sem, h_ready.at(1, 4))
                gate_up(DENSE_AT, 0, 1, tokens, NT, first=True)
                turn(1, NT)
                gate_up(DENSE_AT - 2, 1, 2, tokens, NT)
                down(DENSE_AT + 2, 1, 1, NT, True, False)
                turn(2, NT)
                with pe.Fori(2, DCH) as i:
                    gate_up(DENSE_AT - 2, i, i + 1, tokens, NT)
                    down(DENSE_AT + 2, i, i, NT, False, False)
                    turn(i + 1, NT)
                down(DENSE_AT + 4, DCH - 1, DCH, NT, False, True)

            def route():
                pe.wait_ge(h_ready.sem, h_ready.at(3, 4))
                for t in range(NT):
                    for k in range(KD):
                        for i, h in enumerate((h_hi, h_lo)):
                            last = pe.matmul(ps[:, 6, t * 8:t * 8 + 8], h[:, k, t * P:(t + 1) * P].bitcast(F32),
                                             router[:, k, :], start=(k == 0 and i == 0), stop=(k == KD - 1 and i == 1))
                last.then_inc(logit_done.sem, 1)
                pe.wait_ge(picks_ready.sem, 1)
                mk = rt[:, 2, :]
                pe.matmul(ps[:, 7, 0:8], c("tri"), mk[:, 0:8], start=True, stop=True)
                pe.matmul(ps[:, 7, 8:16], ones, mk[:, 0:8], start=True, stop=False)
                pe.matmul(ps[:, 7, 8:16], c("tri"), mk[:, 8:16], start=False, stop=True)
                pe.matmul(ps[:, 7, 16:24], ones, mk[:, 0:8], start=True, stop=False)
                pe.matmul(ps[:, 7, 16:24], ones, mk[:, 8:16], start=False, stop=True).then_inc(ranks_done.sem, 1)

            def gather(n_sel):
                pe.wait_ge(sel_ready.sem, n_sel)
                for half in range(2):
                    for k in range(4):
                        for t in range(NT):
                            last = pe.matmul(ps[:, 6 + half, k * P:(k + 1) * P],
                                             view(zone, HN + t * D + 4 * half + k, [[KD, P]]), sel[:, t, :],
                                             start=(t == 0), stop=(t == NT - 1))
                    last.then_inc(gathered.sem, 1)

            def expert_up(e, ch):
                if ch == 0:
                    pe.wait_ge(hg_ready.sem, e * 2 + 2)
                gate_up(MOE_AT + (6 * ch - 2 if ch else 0), e * ECH, e * ECH + (DCH + ch + 1),
                        lambda k, t: (hg_hi[:, k, :], hg_lo[:, k, :]), 1)

            def expert_down(e, ch):
                down(MOE_AT + (6 * ch + 8 if ch < ECH - 1 else 6 * ECH - 2), e * ECH, e * ECH + (DCH + ch + 1),
                     1, ch == 0, ch == ECH - 1)

            def expert(e, last_one):
                for ch in range(1, ECH):
                    expert_up(e, ch)
                    expert_down(e, ch - 1)
                    turn(e * ECH + (DCH + ch + 1), 1)
                    if ch == 1:
                        pe.wait_ge(selw_ready.sem, e * 2 + 2)
                        for t in range(NT):
                            last = pe.transpose(ps[:, 6, t * P:(t + 1) * P], sel_w[:, t, :], ident)
                        last.then_inc(selw_turned.sem, 1)
                pe.wait_ge(selwt_ready.sem, e + 1)
                if not last_one:
                    gather(e * 2 + 4)
                expert_down(e, ECH - 1)
                if not last_one:
                    expert_up(e + 1, 0)
                pe.wait_ge(y_ready.sem, e + 1)
                for i in range(4):
                    t, n = divmod(i, 2)
                    if i >= 2:
                        pe.wait_ge(added.sem, e * 4 + (i - 1))
                    pe.matmul(ps[:, 6 + n, :], sel_wt[:, t, :], y_sb[:, n, :], start=True, stop=True
                              ).then_inc(scattered.sem, 1)
                if not last_one:
                    turn(e * ECH + (DCH + ECH + 1), 1)

            def moe_pass(base):
                gather(base * 2 + 2)
                expert_up(base, 0)
                turn(base * ECH + DCH + 1, 1)
                with pe.Fori(base, base + N_EXP - 1) as e:
                    expert(e, False)
                expert(base + N_EXP - 1, True)

            pe.wait_ge(con_landed.sem, 16)
            for layer in range(DEPTH):
                turn_h(2 * layer)
                project(layer)
                attention(layer)
                output_projection(layer)
                turn_h(2 * layer + 1)
                if layer % 2 == 0:
                    dense()
                else:
                    route()
                    pe.wait_ge(over_ready.sem, 1)
                    moe_pass(0)
            more = pe.value_load(over[0:1, 0:1])
            with pe.If(more > 0):
                pe.wait_ge(added.sem, 4 * N_EXP)
                moe_pass(N_EXP)

        @block.scalar
        def _(act):
            act.dma_start(con[:, :], consts_in).then_inc(con_landed.sem, 16)

            def small(dst, src):
                act.dma_start(dst, src).then_inc(small_landed.sem, 16)

            for t in range(NT):
                small(pos_i[:, t:t + 1], pos_in[0, t * P:(t + 1) * P].rearrange("(p o) -> p o", o=1))
            small(g_cq[:, :, :], w["g_cq"].rearrange("l (p k) -> p l k", k=2))
            for layer in range(DEPTH):
                small(g_ckv[:, layer:layer + 1], w["g_ckv"][layer].rearrange("(p o) -> p o", o=1))
            small(sinks[:, :, :], bass.AP(w["a_sinks"].tensor, 0, [[0, P], [1, DEPTH * A_HEADS]]))
            small(router[:, :, :], w["moe_router"][0].rearrange("(p k) e -> p k e", k=KD))

            def square_mean(dst, src, junk, width):
                return act.activation(junk, src, ACT.Square, scale=float(width) ** -0.5, accum_out=dst)

            def split(n, r, words=PIECE):
                act.wait_ge(slot_landed[n % RING].sem, r * 16 + 16 * (n // RING + 1))
                if n >= SPLITS or not isinstance(r, int):
                    wait_piece(act, piece_used, n - SPLITS, r)
                act.activation(w_hi[:, n % SPLITS, 0:words], raw[:, n % RING, 0:words], ACT.Copy
                               ).then_inc(hi_ready.sem, 1)

            def split_w_in(layer, *pieces):
                for i in pieces:
                    if i == LATENT_B:
                        act.wait_ge(gates_landed.sem, gates_landed.at(layer, 16))
                    split(MIXER_AT[layer] + i, 0, KD * W_IN_WIDTH[i])

            def split_rows(b):
                for i in range(4):
                    t, half = divmod(i, 2)
                    act.wait_ge(hn_turned.sem, hn_turned.at(b, i + 1))
                    act.activation(h_hi[:, 4 * half:4 * half + 4, t * P:(t + 1) * P],
                                   ps[:, i, :].rearrange("p (k n) -> p k n", k=4), ACT.Copy).then_inc(hhi_ready.sem, 1)

            def split_mixed(layer, part):
                for t in range(NT):
                    act.wait_ge(mixed_turned.sem, mixed_turned.at(layer, 2 * part + t + 1))
                    act.activation(mix_hi[part][:, :, t * P:(t + 1) * P],
                                   ps[:, 6 * part + t, :].rearrange("p (k n) -> p k n", k=4), ACT.Copy
                                   ).then_inc(mixhi_ready.sem, 1)

            def pre_norm(b):
                for t in range(NT):
                    if b == 0:
                        act.wait_ge(x_landed.sem, 16 * NT)
                    else:
                        act.wait_ge(x_updated.sem, x_updated.at(b - 1, t + 1))
                    square_mean(mean[:, t:t + 1], x[:, t, :], hn[:, t, :], D).then_inc(pre_sq.sem, 1)

            def post_norm(b, src):
                for t in range(NT):
                    square_mean(mean[:, t:t + 1], src(t), hn[:, t, :], D).then_inc(post_sq.sem, 1)

            def mixer(layer):
                def copied(i):
                    wait_piece(act, piece_used, MIXER_AT[layer] + i, 0)

                if layer:
                    split_rows(2 * layer)
                    split_w_in(layer, 2)
                else:
                    split_rows(0)
                    split_w_in(layer, 0, 1, 2)
                split_w_in(layer, 3)
                copied(LATENT_B)
                act.activation(gate[:, 0, :], ps[:, 2, 416:440], ACT.Copy)
                act.activation(bl[:, 0, :], ps[:, 2, 0:416], ACT.Copy).then_inc(proj_out_a.sem, 1)
                act.wait_ge(proj_out_a.sem, proj_out_a.at(layer, 1))
                act.wait_ge(proj_out_d.sem, proj_out_d.at(layer, 1))
                for t in range(NT):
                    square_mean(mean[:, 2 * t:2 * t + 1], bl[:, t, 0:256], hn[:, t, 0:256], 256).then_inc(lat_sq.sem, 1)
                    square_mean(mean[:, 2 * t + 1:2 * t + 2], bl[:, t, 256:384], hn[:, t, 256:384], 128
                                ).then_inc(lat_sq.sem, 1)
                split_w_in(layer, 4)
                copied(CMP_IN)
                for g in range(2):
                    last = act.activation(view(zone, XS + g * S, [[512, 2], [1, S]], 0, 64),
                                          ps[64 * g:64 * g + 64, 6, :].rearrange("p (i n) -> p i n", i=2), ACT.Copy)
                last.then_inc(proj_out_a.sem, 1)
                split_w_in(layer, 5)
                copied(A_Q)
                for h in range(A_HEADS):
                    g, j = divmod(h, 2)
                    last = act.activation(aq_t[64 * g:64 * g + 64, j, :],
                                          ps[64 * (h % 2):64 * (h % 2) + 64, 0, (h // 2) * S:(h // 2 + 1) * S],
                                          ACT.Copy, scale=QK_SCALE)
                last.then_inc(proj_out_a.sem, 1)
                split_w_in(layer, 6, 7)
                if layer == 0:
                    act.wait_ge(sin_ready.sem, 1)
                    act.activation(sincos[:, :, :, :].rearrange("p a t n -> p (a t) n"), ang, ACT.Sin).then_inc(sin_done.sem, 1)
                for t in range(NT):
                    act.wait_ge(latup_done.sem, latup_done.at(layer, 3 + t))
                    act.activation(view(zone, CQN + 1280 + t * 512, [[64, 4], [256, 2], [1, 64]]),
                                   ps[:, LAT_KV_BANKS[t], :].rearrange("p (h i d) -> p h i d", h=4, i=2), ACT.Copy
                                   ).then_inc(kv_out.sem, 1)
                split_w_in(layer, 8)

                def even_queries(g):
                    copied(C_Q0 + g)
                    act.activation(view(zone, Z + 1024, [[512, 2], [1, S]], 64 * g, 64),
                                   ps[0:64, 4 + g, :].rearrange("p (j n) -> p j n", j=2), ACT.Copy, scale=QK_SCALE
                                   ).then_inc(proj_out_a.sem, 1)

                even_queries(0)
                act.wait_ge(gelu_arg.sem, gelu_arg.at(layer, 1))
                act.activation(hid[:, 2, 0:62], hid[:, 1, 0:62], ACT.Exp, scale=-GELU_C).then_inc(gelu_exp.sem, 1)
                act.activation(gate[:, :, :], gate[:, :, :], ACT.Exp, scale=-1.0).then_inc(gates_exp.sem, 1)
                even_queries(1)
                split(MIXER_AT[layer] + N_W_IN, 0)
                for i, bank in ((0, 3), (1, 2), (2, 7)):
                    act.wait_ge(qk_turned.sem, qk_turned.at(layer, i + 1))
                    act.activation(zv(QN_T + 512 * i, 512), ps[:, bank, :], ACT.Copy).then_inc(qk_out.sem, 1)
                copied(SW_KEYS)
                act.activation(view(zone, KS, [[512, 2], [1, S]]), ps[:, 0, :].rearrange("p (b n) -> p b n", b=2), ACT.Copy
                               ).then_inc(proj_out_a.sem, 1)
                act.wait_ge(cs_arg.sem, cs_arg.at(layer, 1))
                act.activation(p_cmp[:, :, 0:N_CMP], p_cmp[:, :, 0:N_CMP], ACT.Exp).then_inc(cs_exp.sem, 1)

                w_o_at = MIXER_AT[layer] + N_W_IN
                for j in range(NJ + 5):
                    if j < NJ:
                        act.wait_ge(max_ready.sem, max_ready.at(layer, j + 1))
                        act.activation(sc_sb[:, j % 5, 0:P], sc_sb[:, j % 5, 0:P], ACT.Exp, bias=nmax[:, j, 0:1],
                                       accum_out=rsum[:, j, 0:1])
                        act.activation(sc_sb[:, j % 5, P:SPAN], sc_sb[:, j % 5, P:SPAN], ACT.Exp, bias=nmax[:, j, 1:2],
                                       accum_out=rsum[:, j, 1:2]).then_inc(probs_ready.sem, 1)
                    if j == 5:
                        act.wait_ge(sink_arg.sem, sink_arg.at(layer, 1))
                        act.activation(sink_e[:, :, :], sink_e[:, :, :], ACT.Exp).then_inc(sink_exp.sem, 1)
                    i = j - 3
                    if i >= 0 and i < NJ:
                        act.wait_ge(probs_turned.sem, probs_turned.at(layer, i + 1))
                        if i >= 2:
                            act.wait_ge(pv_done.sem, pv_done.at(layer, i - 1))
                        act.activation(pt[:, i % 2, :], ps[:, 2 + i % 2, 0:SPAN], ACT.Copy).then_inc(pt_ready.sem, 1)
                    if j in (8, 12):
                        split(w_o_at + j // 4 - 1, 0)
                    if j >= 6 and j % 2 == 0:
                        p = (j - 6) // 2
                        act.wait_ge(pv_done.sem, pv_done.at(layer, 2 * p + 2))
                        if p >= 2:
                            act.wait_ge(turned_back.sem, turned_back.at(layer, p - 1))
                        act.activation(o_t[:, p % 2, :], ps[:, 4 + p % 2, 0:S], ACT.Copy).then_inc(ot_ready.sem, 1)
                    if j == 16:
                        act.wait_ge(o_out.sem, o_out.at(layer, 2))
                        for t in range(NT):
                            for g in range(2):
                                at = 2 * t + g
                                square_mean(mean[:, at:at + 1], o_all[:, t, g * 256:(g + 1) * 256],
                                            zv(ROPE_IN + 256 * at, 256), 256).then_inc(o_sq.sem, 1)
                    if j == 26:
                        split_mixed(layer, 0)
                act.wait_ge(o_out.sem, o_out.at(layer, 4))
                for t in range(NT):
                    square_mean(mean[:, 4 + t:5 + t], o_all[:, t, 512:1024], hn[:, t, 0:512], 512).then_inc(o_sq.sem, 1)
                split_mixed(layer, 1)
                for i in range(3, 6):
                    split(w_o_at + i, 0)
                wait_piece(act, piece_used, w_o_at + 3, 0)
                act.wait_ge(mixed_ready.sem, mixed_ready.at(layer, 2))
                post_norm(2 * layer, lambda t: ps[:, 2 * t:2 * t + 2, :])

            def silu(n, r, step, tiles, first=False):
                wait_piece(act, piece_used, n, r)
                if not first:
                    act.wait_ge(act_turned.sem, step - 1)
                act.activation(sil[:, 0:tiles, :], ps[:, 0:tiles, :], ACT.Silu).then_inc(silu_ready.sem, 1)

            def split_act(step, tiles):
                act.wait_ge(act_turned.sem, step)
                act.activation(act_hi[:, 0:tiles, :], ps[:, 2:2 + tiles, :], ACT.Copy).then_inc(acthi_ready.sem, 1)

            def chunk(at, r, step, tiles, tail=6):
                split(at + 4, r)
                silu(at + 1, r, step, tiles)
                for i in (5, 6, 7):
                    if i < tail:
                        split(at + i, r)
                split_act(step, tiles)
                for i in (8, 9):
                    if i < tail:
                        split(at + i, r)

            for layer in range(DEPTH):
                pre_norm(2 * layer)
                mixer(layer)
                pre_norm(2 * layer + 1)
                b0 = (DENSE_AT, MOE_AT)[layer]
                split_rows(2 * layer + 1)
                split(b0 + 2, 0)
                if layer % 2 == 0:
                    split(DENSE_AT + 3, 0)
                    split(DENSE_AT + 4, 0)
                    silu(DENSE_AT + 1, 0, 1, NT, first=True)
                    split(DENSE_AT + 5, 0)
                    split(DENSE_AT + 6, 0)
                    split_act(1, NT)
                    split(DENSE_AT + 7, 0)
                    with act.Fori(1, DCH - 1) as i:
                        chunk(DENSE_AT - 2, i, i + 1, NT, tail=10)
                    chunk(DENSE_AT - 2, DCH - 1, DCH, NT, tail=8)
                    split_w_in(1, 0, 1)
                    wait_piece(act, piece_used, DENSE_AT + 6 * DCH - 1, 0)
                    post_norm(1, lambda t: ps[:, 4 + 2 * t:6 + 2 * t, :])
                else:
                    act.wait_ge(route_arg.sem, 1)
                    act.activation(rt[:, 10, 0:2], rt[:, 9, 0:2], ACT.Exp).then_inc(route_exp.sem, 1)

            def split_gathered(e):
                for half in range(2):
                    act.wait_ge(gathered.sem, e * 2 + (half + 1))
                    act.activation(hg_hi[:, 4 * half:4 * half + 4, :],
                                   ps[:, 6 + half, :].rearrange("p (k n) -> p k n", k=4), ACT.Copy
                                   ).then_inc(hghi_ready.sem, 1)

            def expert(e, last_one):
                r = e * ECH
                for ch in range(1, ECH - 1):
                    chunk(MOE_AT + 6 * ch - 2, r, e * ECH + (DCH + ch + 1), 1, tail=10)
                at, step = MOE_AT + 6 * ECH - 8, e * ECH + (DCH + ECH)
                chunk(at, r, step, 1, tail=8)
                if not last_one:
                    split_gathered(e + 1)
                    for i in (8, 9, 10):
                        split(at + i, r)
                wait_piece(act, piece_used, at + 7, r)
                act.activation(y_sb, ps[:, 4:6, :], ACT.Copy).then_inc(y_ready.sem, 1)
                if not last_one:
                    split(at + 11, r)
                    split(at + 12, r)
                    silu(at + 9, r, e * ECH + (DCH + ECH + 1), 1)
                    split(at + 13, r)
                    split(at + 14, r)
                    split_act(e * ECH + (DCH + ECH + 1), 1)
                    split(at + 15, r)

            def moe_pass(base, second):
                r, step = base * ECH, base * ECH + DCH + 1
                if second:
                    for i in range(3):
                        split(MOE_AT + i, r)
                split_gathered(base)
                for i in (3, 4):
                    split(MOE_AT + i, r)
                silu(MOE_AT + 1, r, step, 1)
                for i in (5, 6):
                    split(MOE_AT + i, r)
                split_act(step, 1)
                split(MOE_AT + 7, r)
                with act.Fori(base, base + N_EXP - 1) as e:
                    expert(e, False)
                expert(base + N_EXP - 1, True)

            moe_pass(0, False)
            act.wait_ge(over_ready.sem, 1)
            more = act.value_load(over[0:1, 0:1])
            with act.If(more > 0):
                moe_pass(N_EXP, True)
            act.wait_ge(f_summed.sem, 1)
            post_norm(3, lambda t: f_acc[:, t, :])

        @block.vector
        def _(dve):
            chain = [0]

            def link(ins):
                chain[0] += 1
                ins.then_inc(dve_chain.sem, 1)
                dve.wait_ge(dve_chain.sem, chain[0])

            def rest(n, r, words=PIECE):
                wait_piece(dve, hi_ready, n, r)
                dve.tensor_tensor(w_lo[:, n % SPLITS, 0:words], raw[:, n % RING, 0:words],
                                  w_hi[:, n % SPLITS, 0:words].bitcast(F32), ALU.subtract).then_inc(lo_ready.sem, 1)

            def rest_rows(b):
                for i in range(4):
                    t, half = divmod(i, 2)
                    part = (slice(None), slice(4 * half, 4 * half + 4), slice(t * P, (t + 1) * P))
                    dve.wait_ge(hhi_ready.sem, hhi_ready.at(b, i + 1))
                    dve.tensor_tensor(h_lo[part], ps[:, i, :].rearrange("p (k n) -> p k n", k=4),
                                      h_hi[part].bitcast(F32), ALU.subtract).then_inc(h_ready.sem, 1)

            def rest_mixed(layer, part):
                for t in range(NT):
                    cols = (slice(None), slice(None), slice(t * P, (t + 1) * P))
                    dve.wait_ge(mixhi_ready.sem, mixhi_ready.at(layer, 2 * part + t + 1))
                    dve.tensor_tensor(mix_lo[part][cols], ps[:, 6 * part + t, :].rearrange("p (k n) -> p k n", k=4),
                                      mix_hi[part][cols].bitcast(F32), ALU.subtract).then_inc(mix_ready.sem, 1)

            def norm_group(t, a, n, factor):
                o = o_all[:, t, a:a + n]
                return dve.scalar_tensor_tensor(out=o, in0=o, scalar=rstd[:, factor:factor + 1], in1=g_in[:, a:a + n],
                                                op0=ALU.mult, op1=ALU.mult)

            def pre_norm(b):
                dve.wait_ge(gin_landed.sem, gin_landed.at(b // 2, 80 if b % 2 else 16))
                for t in range(NT):
                    dve.wait_ge(pre_rstd.sem, pre_rstd.at(b, t + 1))
                    dve.scalar_tensor_tensor(out=hn[:, t, :], in0=x[:, t, :], scalar=rstd[:, t:t + 1], in1=g_in[:, :],
                                             op0=ALU.mult, op1=ALU.mult).then_inc(hn_ready.sem, 1)
                rest_rows(b)

            def post_norm(b, src):
                dve.wait_ge(gpost_landed.sem, gpost_landed.at(b, 16))
                for t in range(NT):
                    dve.wait_ge(post_rstd.sem, post_rstd.at(b, t + 1))
                    hv = hn[:, t, :].rearrange("p (n c) -> p n c", n=2)
                    link(dve.scalar_tensor_tensor(out=hv, in0=src(t), scalar=rstd[:, t:t + 1],
                                                  in1=g_post[:, :].rearrange("p (n c) -> p n c", n=2),
                                                  op0=ALU.mult, op1=ALU.mult))
                    dve.tensor_tensor(x[:, t, :], x[:, t, :], hn[:, t, :], ALU.add).then_inc(x_updated.sem, 1)

            def rest_w_in(i, layer):
                rest(MIXER_AT[layer] + i, 0, KD * W_IN_WIDTH[i])

            def mixer(layer):
                def projected(i):
                    wait_piece(dve, piece_used, MIXER_AT[layer] + i, 0)

                if layer == 0:
                    rest_w_in(0, layer)
                    rest_w_in(1, layer)
                rest_w_in(2, layer)
                rest_w_in(3, layer)
                projected(LATENT_B)
                dve.tensor_copy(gate[:, 1, :], ps[:, 3, 416:440])
                dve.tensor_copy(bl[:, 1, :], ps[:, 3, 0:416]).then_inc(proj_out_d.sem, 1)
                dve.wait_ge(lat_rstd.sem, lat_rstd.at(layer, 1))
                for t in range(NT):
                    for i, (a, n) in enumerate(((0, 256), (256, 128))):
                        last = dve.tensor_scalar(bl[:, t, a:a + n], bl[:, t, a:a + n], rstd[:, 2 * t + i:2 * t + i + 1],
                                                 None, ALU.mult)
                last.then_inc(lat_ready.sem, 1)
                rest_w_in(4, layer)
                projected(CMP_IN)
                dve.wait_ge(proj_out_a.sem, proj_out_a.at(layer, 2))
                for g in range(2):
                    last = dve.tensor_copy(view(zone, XS + g * S, [[512, 2], [1, 255]], 64, 64),
                                           view(ps, 6 * 512 + 1, [[256, 2], [1, 255]], 64 * g, 64))
                last.then_inc(proj_out_d.sem, 1)
                rest_w_in(5, layer)
                if layer == 0:
                    dve.wait_ge(con_landed.sem, 16)
                    dve.wait_ge(small_landed.sem, 16 * N_SMALL)
                    rotary_setup()
                dve.wait_ge(pe_turned.sem, pe_turned.at(layer, 1))
                link(dve.tensor_copy(pe_t[:, :, :], ps[:, 7, 0:32].rearrange("p (i a) -> p i a", i=2)))
                dve.wait_ge(proj_out_d.sem, proj_out_d.at(layer, 2))
                dve.wait_ge(lat_sq.sem, lat_sq.at(layer, 4))
                for i in range(2):
                    for g in range(2):
                        last = dve.tensor_tensor(view(zone, HN + i * 480 + g * 15, [[30, 16], [1, 15]]),
                                                 view(zone, XS + i * 512 + g * 256, [[2, 16], [16, 15]]),
                                                 view(pe_t, i * 16, [[1, 16], [0, 15]]), ALU.add)
                    last.then_inc(blk_ready.sem, 1)
                dve.wait_ge(lat_turned.sem, lat_turned.at(layer, 1))
                dve.tensor_tensor(cqn_t[:, 0:2, :], ps[:, 3, :].rearrange("p (k n) -> p k n", k=2),
                                  view(g_cq, layer * 2, [[1, 2], [0, S]]), ALU.mult).then_inc(latt_ready.sem, 1)
                dve.wait_ge(lat_turned.sem, lat_turned.at(layer, 2))
                dve.tensor_scalar(cqn_t[:, 2, :], ps[:, 2, 0:S], g_ckv[:, layer:layer + 1], None, ALU.mult
                                  ).then_inc(latt_ready.sem, 1)
                rest_w_in(6, layer)
                projected(A_KEYS)
                dve.tensor_copy(akv, ps[:, 1, :]).then_inc(proj_out_d.sem, 1)
                rest_w_in(7, layer)
                if layer == 0:
                    dve.wait_ge(sin_done.sem, 1)
                for t in range(NT):
                    dve.wait_ge(latup_done.sem, latup_done.at(layer, t + 1))
                    bank = 4 + t
                    dve.tensor_copy(view(zone, CQN + 768 + t * 256, [[64, 4], [1, 64]]),
                                    view(ps, bank * 512, [[96, 4], [1, 64]]))
                    dve.tensor_copy(view(zone, ROPE_IN + t * 160, [[32, 4], [1, 32]]),
                                    view(ps, bank * 512 + 64, [[96, 4], [1, 32]])).then_inc(latup_out.sem, 1)
                    link(dve.tensor_copy(view(zone, ROPE_IN + t * 160 + 128, [[1, 32]]), bl[:, t, 384:416]))
                    rope_in = view(zone, ROPE_IN + t * 160, [[32, 5], [16, 2], [1, 16]])
                    cos = view(sincos, 32 + t * 16, [[0, 5], [0, 2], [1, 16]])
                    sin = view(sincos, t * 16, [[0, 5], [0, 2], [1, 16]])
                    dve.tensor_tensor(view(zone, ROPE_A + t * 160, [[32, 5], [16, 2], [1, 16]]), rope_in, cos, ALU.mult)
                    link(dve.tensor_tensor(view(zone, ROPE_B + t * 160, [[32, 5], [16, 2], [1, 16]]), rope_in, sin,
                                           ALU.mult))
                    for half, op in ((0, ALU.subtract), (1, ALU.add)):
                        dve.tensor_tensor(view(zone, ROPE_O + t * P + half * 16, [[32, 4], [1, 16]]),
                                          view(zone, ROPE_A + t * 160 + half * 16, [[32, 4], [1, 16]]),
                                          view(zone, ROPE_B + t * 160 + (1 - half) * 16, [[32, 4], [1, 16]]), op)
                        last = dve.tensor_tensor(view(zone, ROPE_O + S + t * P + half * 16, [[32, 4], [1, 16]]),
                                                 view(zone, ROPE_A + t * 160 + 128 + half * 16, [[0, 4], [1, 16]]),
                                                 view(zone, ROPE_B + t * 160 + 128 + (1 - half) * 16, [[0, 4], [1, 16]]),
                                                 op)
                last.then_inc(qk_ready.sem, 1)
                dve.wait_ge(qk_ready.sem, qk_ready.at(layer, 1))
                dve.wait_ge(hid_done.sem, hid_done.at(layer, 2))
                link(dve.tensor_copy(hid[:, 0, 0:62], ps[:, 6, 0:62]))
                link(dve.tensor_tensor(hid[:, 1, 0:62], hid[:, 0, 0:62], hid[:, 0, 0:62], ALU.mult))
                link(dve.tensor_scalar(hid[:, 1, 0:62], hid[:, 1, 0:62], 0.044715, 1.0, ALU.mult, ALU.add))
                dve.tensor_tensor(hid[:, 1, 0:62], hid[:, 1, 0:62], hid[:, 0, 0:62], ALU.mult).then_inc(gelu_arg.sem, 1)
                link(dve.memset(p_cmp, 0.0))
                rest_w_in(8, layer)

                def odd_queries(g):
                    projected(C_Q0 + g)
                    dve.tensor_scalar(view(zone, Z + 1024 + 256, [[512, 2], [1, S]], 64 * g, 64),
                                      ps[64:128, 4 + g, :].rearrange("p (j n) -> p j n", j=2), QK_SCALE, None, ALU.mult
                                      ).then_inc(proj_out_d.sem, 1)

                odd_queries(0)
                dve.wait_ge(gelu_exp.sem, gelu_exp.at(layer, 1))
                link(dve.tensor_scalar(hid[:, 2, 0:62], hid[:, 2, 0:62], 1.0, None, ALU.add))
                link(dve.reciprocal(hid[:, 3, 0:62], hid[:, 2, 0:62]))
                dve.tensor_tensor(hid[:, 0, 0:62], hid[:, 0, 0:62], hid[:, 3, 0:62], ALU.mult
                                  ).then_inc(gelu_ready.sem, 1)
                odd_queries(1)
                dve.wait_ge(gates_exp.sem, gates_exp.at(layer, 1))
                link(dve.tensor_scalar(gate[:, :, :], gate[:, :, :], 1.0, None, ALU.add))
                link(dve.reciprocal(gate[:, :, :], gate[:, :, :]))
                rest(MIXER_AT[layer] + N_W_IN, 0)
                link(dve.memset(v_cmp, 0.0))
                dve.wait_ge(ckv_done.sem, ckv_done.at(layer, 2))
                dve.tensor_copy(kc_t[:, 0:N_CMP], ps[:, 6, 64:64 + N_CMP])
                for i in range(4):
                    last = dve.tensor_copy(v_cmp[32 * i:32 * i + N_CMP, :, HEAD * i:HEAD * (i + 1)],
                                           ps[32 * i:32 * i + N_CMP, 6, 128:256].rearrange("p (g d) -> p g d", g=2))
                last.then_inc(ckv_out.sem, 1)
                dve.wait_ge(cs_done.sem, cs_done.at(layer, 1))
                for h in range(C_HEADS):
                    last = dve.scalar_tensor_tensor(out=view(zone, ROPE_IN + h * 32, [[256, NT], [1, N_CMP]]),
                                                    in0=c("dist_cmp").rearrange("p (t n) -> p t n", t=NT),
                                                    scalar=C_SLOPES[h],
                                                    in1=view(ps, (6 + h // 4) * 512 + h % 4 * 16, [[64, NT], [1, N_CMP]]),
                                                    op0=ALU.mult, op1=ALU.add)
                link(last)
                link(dve.tensor_reduce(cmax[:, :], p_cmp[:, :, 0:N_CMP], AX_X, ALU.max, negate=True))
                dve.tensor_tensor(p_cmp[:, :, 0:N_CMP], p_cmp[:, :, 0:N_CMP], view(cmax, 0, [[1, 16], [0, N_CMP]]), ALU.add
                                  ).then_inc(cs_arg.sem, 1)
                projected(SW_VALUES)
                dve.tensor_copy(view(zone, KS + S, [[512, 2], [P, 2], [1, P]]), view(ps, 512, [[P, 2], [256, 2], [1, P]])
                                ).then_inc(proj_out_d.sem, 1)

                def gated(branch, r, first):
                    for t in range(NT):
                        g = view(gate, t * 24 + branch, [[3, 8]])
                        if first:
                            a, _ = COL["has_cmp"]
                            link(dve.scalar_tensor_tensor(out=gscale[:, t, :], in0=r(t), scalar=con[:, a + t:a + t + 1],
                                                          in1=g, op0=ALU.mult, op1=ALU.mult))
                        else:
                            link(dve.tensor_tensor(gscale[:, t, :], r(t), g, ALU.mult))
                    for t in range(NT):
                        src = ps[:, 6 + t, :].rearrange("p (h d) -> p h d", h=8)
                        fac = view(gscale, t * 8, [[1, 8], [0, HEAD]])
                        dst = o_all[:, t, 512:1024]
                        if first:
                            last = dve.tensor_tensor(dst.rearrange("p (h d) -> p h d", h=8), src, fac, ALU.mult)
                        else:
                            link(dve.tensor_tensor(c_tmp.rearrange("p (h d) -> p h d", h=8), src, fac, ALU.mult))
                            last = dve.tensor_tensor(dst, dst, c_tmp, ALU.add)
                            if t == 0:
                                link(last)
                    return last

                def copy_o(kind, j0):
                    for t in range(NT):
                        col = 0 if kind == "A" else 256
                        last = dve.tensor_tensor(o_all[:, t, col:col + 256].rearrange("p (h d) -> p h d", h=4),
                                                 ps[:, 6 + t, col:col + 256].rearrange("p (h d) -> p h d", h=4),
                                                 view(rinv, j0 * 2 + t, [[2, 4], [0, HEAD]]), ALU.mult)
                    return last

                w_o_at = MIXER_AT[layer] + N_W_IN
                for j in range(NJ + 3):
                    if j < NJ:
                        kind, h = JOBS[j]
                        dve.wait_ge(score_done.sem, score_done.at(layer, j + 1))
                        if j >= 5:
                            dve.wait_ge(probs_turned.sem, probs_turned.at(layer, j - 4))
                        s = sc_sb[:, j % 5, :]
                        raw = ps[:, j % 2, 0:SPAN]
                        if kind == "B":
                            ins = dve.scalar_tensor_tensor(out=s, in0=raw, scalar=B_SCALE, in1=c("mask_b"),
                                                           op0=ALU.mult, op1=ALU.add)
                        else:
                            ins = dve.scalar_tensor_tensor(out=s, in0=c("dist_a" if kind == "A" else "dist_c"),
                                                           scalar=(A_SLOPES if kind == "A" else C_SLOPES)[h],
                                                           in1=raw, op0=ALU.mult, op1=ALU.add)
                        ins.then_inc(biased.sem, 1)
                        dve.wait_ge(biased.sem, biased.at(layer, j + 1))
                        dve.tensor_reduce(nmax[:, j, 0:1], s[:, 0:P], AX_X, ALU.max, negate=True)
                        ins = dve.tensor_reduce(nmax[:, j, 1:2], s[:, P:SPAN], AX_X, ALU.max, negate=True)
                        if kind == "A":
                            link(ins)
                            ins = dve.tensor_scalar(nmax[:, j, :], nmax[:, j, :], neg_sinks[:, layer, h:h + 1], None,
                                                    ALU.min)
                        ins.then_inc(max_ready.sem, 1)
                    if j == 0:
                        dve.wait_ge(cp_turned.sem, cp_turned.at(layer, 1))
                        dve.tensor_copy(pt_cmp, ps[:, 2, :].rearrange("p (a b) -> p a b", b=P)).then_inc(cp_out.sem, 1)
                        link(dve.tensor_reduce(csum[:, :], p_cmp[:, :, 0:N_CMP], AX_X, ALU.add))
                        link(dve.reciprocal(csum[:, :], csum[:, :]))
                    if j == 2:
                        dve.wait_ge(co_done.sem, co_done.at(layer, 1))
                        gated(0, lambda t: csum[:, t * 8:t * 8 + 8], True).then_inc(co_out.sem, 1)
                    if j == 4:
                        dve.wait_ge(max_ready.sem, max_ready.at(layer, 4))
                        dve.tensor_tensor(sink_e[:, :, :], nmax[:, 0:4, :], view(sinks, layer * 4, [[1, 4], [0, 2]]), ALU.add
                                          ).then_inc(sink_arg.sem, 1)
                    if j == 9:
                        dve.wait_ge(sink_exp.sem, sink_exp.at(layer, 1))
                        link(dve.tensor_tensor(rsum[:, 0:4, :], rsum[:, 0:4, :], sink_e[:, :, :], ALU.add))
                        link(dve.reciprocal(rinv[:, 0:4, :], rsum[:, 0:4, :]))
                    if j == 14:
                        dve.wait_ge(turned_back.sem, turned_back.at(layer, 4))
                        link(dve.reciprocal(rinv[:, 4:8, :], rsum[:, 4:8, :]))
                        copy_o("A", 0).then_inc(o_out.sem, 1)
                        copy_o("B", 4).then_inc(o_out.sem, 1)
                    if j in (10, 16):
                        rest(w_o_at + 1 + j // 16, 0)
                    if j == 18:
                        dve.wait_ge(gin_landed.sem, gin_landed.at(layer, 64))
                        dve.wait_ge(o_rstd.sem, o_rstd.at(layer, 1))
                        for t in range(NT):
                            for g in range(2):
                                last = norm_group(t, g * 256, 256, 2 * t + g)
                        last.then_inc(mixed_ready.sem, 1)
                    if j == 22:
                        dve.wait_ge(turned_back.sem, turned_back.at(layer, 8))
                        link(dve.reciprocal(rinv[:, 8:16, :], rsum[:, 8:16, :]))
                        gated(1, lambda t: view(rinv, 16 + t, [[2, 8]]), False).then_inc(o_out.sem, 1)
                rest_mixed(layer, 0)
                dve.wait_ge(o_out.sem, o_out.at(layer, 3))
                dve.wait_ge(turned_back.sem, turned_back.at(layer, NJ // 2))
                link(dve.reciprocal(rinv[:, 16:24, :], rsum[:, 16:24, :]))
                gated(2, lambda t: view(rinv, 32 + t, [[2, 8]]), False).then_inc(o_out.sem, 1)
                dve.wait_ge(o_rstd.sem, o_rstd.at(layer, 2))
                for t in range(NT):
                    last = norm_group(t, 512, 512, 4 + t)
                last.then_inc(mixed_ready.sem, 1)
                rest_mixed(layer, 1)
                for i in range(3, 6):
                    rest(w_o_at + i, 0)
                post_norm(2 * layer, lambda t: ps[:, 2 * t:2 * t + 2, :])

            def product(n, r, step, tiles):
                wait_piece(dve, piece_used, n, r)
                dve.wait_ge(silu_ready.sem, step)
                dve.tensor_tensor(sil[:, 0:tiles, :], sil[:, 0:tiles, :], ps[:, 2:2 + tiles, :], ALU.mult
                                  ).then_inc(prod_ready.sem, 1)

            def rest_act(step, tiles):
                dve.wait_ge(acthi_ready.sem, step)
                dve.tensor_tensor(act_lo[:, 0:tiles, :], ps[:, 2:2 + tiles, :],
                                  act_hi[:, 0:tiles, :].bitcast(F32), ALU.subtract).then_inc(act_ready.sem, 1)

            def chunk(at, r, step, tiles, tail=12):
                product(at + 3, r, step, tiles)
                for i in (6, 7):
                    rest(at + i, r)
                rest_act(step, tiles)
                for i in range(8, tail):
                    rest(at + i, r)

            def rotary_setup():
                link(dve.tensor_copy(pos_f[:, :], pos_i[:, :]))
                dve.tensor_scalar(neg_sinks[:, :, :], sinks[:, :, :], -1.0, None, ALU.mult)
                for t in range(NT):
                    for i in range(2):
                        last = dve.tensor_scalar(ang[:, i * NT + t, :], c("inv_freq"), pos_f[:, t:t + 1], None, ALU.mult)
                link(last)
                dve.tensor_scalar(turns[:, 0:NT, :], ang[:, 0:NT, :], 1.0 / TWO_PI, None, ALU.mult)
                link(dve.tensor_scalar(turns[:, NT:, :], ang[:, NT:, :], 1.0 / TWO_PI, 0.25, ALU.mult, ALU.add))
                link(dve.tensor_scalar(turns, turns, ROUND, None, ALU.add))
                link(dve.tensor_scalar(turns, turns, ROUND, None, ALU.subtract))
                a2, t2 = (v.rearrange("p a n -> p (a n)") for v in (ang, turns))
                for part in (PI_1, PI_2, PI_3):
                    link(dve.scalar_tensor_tensor(out=a2, in0=t2, scalar=-part, in1=a2, op0=ALU.mult, op1=ALU.add))
                link(dve.tensor_scalar(ang[:, NT:, :], ang[:, NT:, :], float(np.pi / 2), None, ALU.add))
                dve.tensor_scalar(a2, a2, SIN_MAX, -SIN_MAX, ALU.min, ALU.max).then_inc(sin_ready.sem, 1)

            def pick(logits, scratch, chosen, top):
                link(dve.tensor_reduce(top, logits, AX_X, ALU.max))
                topb = bass.AP(top.tensor, top.offset, [list(top.ap[0]), list(top.ap[1]), [0, 8]])
                link(dve.tensor_tensor(scratch, logits, topb, ALU.is_ge))
                a, _ = COL["iota"]
                iota8 = view(con, a, [[0, NT], [1, 8]])
                link(dve.tensor_scalar(scratch, scratch, -8.0, 8.0, ALU.mult, ALU.add))
                link(dve.tensor_tensor(scratch, scratch, iota8, ALU.add))
                link(dve.tensor_reduce(cnt[:, 0:2], scratch, AX_X, ALU.min))
                link(dve.tensor_tensor(chosen, iota8, view(cnt, 0, [[1, NT], [0, 8]]), ALU.is_equal))

            def route():
                link(dve.memset(ones, 1.0))

                def r(i):
                    return rt[:, i, :].rearrange("p (t e) -> p t e", t=NT)

                dve.wait_ge(logit_done.sem, 1)
                link(dve.tensor_copy(rt[:, 0, :], ps[:, 6, 0:16]))
                m1, m2 = rt[:, 7, 0:2], rt[:, 8, 0:2]
                pick(r(0), r(5), r(3), m1)
                link(dve.scalar_tensor_tensor(out=rt[:, 1, :], in0=rt[:, 3, :], scalar=-1e38, in1=rt[:, 0, :],
                                              op0=ALU.mult, op1=ALU.add))
                pick(r(1), r(5), r(4), m2)
                link(dve.tensor_tensor(rt[:, 2, :], rt[:, 3, :], rt[:, 4, :], ALU.add))
                dve.tensor_tensor(rt[:, 9, 0:2], m2, m1, ALU.subtract).then_inc(route_arg.sem, 1)
                dve.engine_nop().then_inc(picks_ready.sem, 1)
                dve.wait_ge(route_exp.sem, 1)
                link(dve.tensor_scalar(rt[:, 9, 2:4], rt[:, 10, 0:2], 1.0, None, ALU.add))
                link(dve.reciprocal(rt[:, 9, 4:6], rt[:, 9, 2:4]))
                link(dve.tensor_tensor(rt[:, 9, 6:8], rt[:, 9, 4:6], rt[:, 10, 0:2], ALU.mult))
                link(dve.tensor_tensor(r(3), r(3), view(rt, 9 * 16 + 4, [[1, NT], [0, 8]]), ALU.mult))
                link(dve.tensor_tensor(r(4), r(4), view(rt, 9 * 16 + 6, [[1, NT], [0, 8]]), ALU.mult))
                link(dve.tensor_tensor(rt[:, 5, :], rt[:, 3, :], rt[:, 4, :], ALU.add))
                dve.wait_ge(ranks_done.sem, 1)
                link(dve.tensor_tensor(rt[:, 6, :], ps[:, 7, 0:16], rt[:, 2, :], ALU.mult))
                link(dve.tensor_scalar(rt[:, 6, :], rt[:, 6, :], -1.0, None, ALU.add))
                link(dve.tensor_reduce(cnt[:, 0:1], ps[:, 7, 16:24], AX_X, ALU.max))
                dve.tensor_scalar(over[:, :], cnt[:, 0:1], float(P), None, ALU.is_gt).then_inc(over_ready.sem, 1)

            def select(e):
                for t in range(NT):
                    dve.tensor_scalar(sel[:, t, :], c("iota"), rt[:, 6, bass.ds(e + t * 8, 1)], None, ALU.is_equal
                                      ).then_inc(sel_ready.sem, 1)

            def expert(e, ei, last_one):
                r = e * ECH
                for t in range(NT):
                    dve.tensor_scalar(sel_w[:, t, :], c("iota"), rt[:, 6, bass.ds(ei + t * 8, 1)],
                                      rt[:, 5, bass.ds(ei + t * 8, 1)], ALU.is_equal, ALU.mult).then_inc(selw_ready.sem, 1)
                if not last_one:
                    select(ei + 1)
                for ch in range(1, ECH - 1):
                    chunk(MOE_AT + 6 * ch - 2, r, e * ECH + (DCH + ch + 1), 1)
                    if ch == 1:
                        dve.wait_ge(selw_turned.sem, e + 1)
                        dve.tensor_copy(sel_wt, ps[:, 6, 0:S].rearrange("p (t n) -> p t n", t=NT)
                                        ).then_inc(selwt_ready.sem, 1)
                at = MOE_AT + 6 * ECH - 8
                chunk(at, r, e * ECH + (DCH + ECH), 1, tail=8)
                step = e * ECH + (DCH + ECH + 1)
                if not last_one:
                    take_gathered(e + 1)
                    for i in range(8, 14):
                        rest(at + i, r)
                    product(at + 11, r, step, 1)
                    rest(at + 14, r)
                for i in range(4):
                    t, n = divmod(i, 2)
                    dve.wait_ge(scattered.sem, e * 4 + (i + 1))
                    f = f_acc[:, t, n * 512:(n + 1) * 512]
                    dve.tensor_tensor(f, f, ps[:, 6 + n, :], ALU.add).then_inc(added.sem, 1)
                if not last_one:
                    rest_act(step, 1)
                    for i in range(15, 18):
                        rest(at + i, r)

            def take_gathered(e):
                for half in range(2):
                    dve.wait_ge(hghi_ready.sem, e * 2 + (half + 1))
                    dve.tensor_tensor(hg_lo[:, 4 * half:4 * half + 4, :],
                                      ps[:, 6 + half, :].rearrange("p (k n) -> p k n", k=4),
                                      hg_hi[:, 4 * half:4 * half + 4, :].bitcast(F32), ALU.subtract
                                      ).then_inc(hg_ready.sem, 1)

            def moe_pass(base):
                r, step = base * ECH, base * ECH + DCH + 1
                select(0)
                if base:
                    for i in range(3):
                        rest(MOE_AT + i, r)
                take_gathered(base)
                for i in (3, 4, 5):
                    rest(MOE_AT + i, r)
                product(MOE_AT + 3, r, step, 1)
                rest(MOE_AT + 6, r)
                rest_act(step, 1)
                for i in (7, 8, 9):
                    rest(MOE_AT + i, r)
                with dve.Fori(base, base + N_EXP - 1) as e:
                    expert(e, e - base if base else e, False)
                expert(base + N_EXP - 1, N_EXP - 1, True)

            for layer in range(DEPTH):
                pre_norm(2 * layer)
                mixer(layer)
                b0 = (DENSE_AT, MOE_AT)[layer]
                pre_norm(2 * layer + 1)
                rest(b0 + 2, 0)
                if layer % 2 == 0:
                    for i in (3, 4, 5):
                        rest(DENSE_AT + i, 0)
                    product(DENSE_AT + 3, 0, 1, NT)
                    rest(DENSE_AT + 6, 0)
                    rest_act(1, NT)
                    for i in (7, 8, 9):
                        rest(DENSE_AT + i, 0)
                    with dve.Fori(1, DCH - 1) as i:
                        chunk(DENSE_AT - 2, i, i + 1, NT)
                    chunk(DENSE_AT - 2, DCH - 1, DCH, NT, tail=8)
                    rest_w_in(0, 1)
                    rest_w_in(1, 1)
                    post_norm(1, lambda t: ps[:, 4 + 2 * t:6 + 2 * t, :])
            route()
            dve.memset(f_acc, 0.0).then_inc(f_zeroed.sem, 1)
            dve.wait_ge(f_zeroed.sem, 1)
            dve.wait_ge(over_ready.sem, 1)
            more = dve.value_load(over[0:1, 0:1])
            moe_pass(0)
            with dve.If(more > 0):
                dve.tensor_scalar(rt[:, 6, :], rt[:, 6, :], -float(P), None, ALU.add).then_inc(slots_shifted.sem, 1)
                dve.wait_ge(slots_shifted.sem, 1)
                moe_pass(N_EXP)
            dve.engine_nop().then_inc(f_summed.sem, 1)
            post_norm(3, lambda t: f_acc[:, t, :].rearrange("p (n c) -> p n c", n=2))


N_SMALL = NT + 1 + DEPTH + 2

_INS = ['x', 'positions', 'w_in', 'a_sinks', 'g_cq', 'w_uq', 'g_ckv', 'w_ukv', 'c_w1_k', 'c_w2_k', 'c_pe_k',
        'c_w1_v', 'c_w2_v', 'c_pe_v', 'g_oa', 'g_ob', 'g_oc', 'w_o', 'g_pre_mix', 'g_post_mix', 'g_pre_ffn',
        'g_post_ffn', 'ffn_w_gate', 'ffn_w_up', 'ffn_w_down', 'moe_router', 'moe_w_gate', 'moe_w_up', 'moe_w_down']


def kernel(**inputs):
    import concourse.bacc as _bacc
    from concourse.bass_utils import run_bass_kernel_spmd as _run

    nc = _bacc.Bacc("TRN2", target_bir_lowering=False, num_devices=1)
    arrays, aps = {}, {}

    def given(name, a):
        arrays[f"in_{name}_dram"] = a
        aps[name] = nc.dram_tensor(f"in_{name}_dram", a.shape, mybir.dt.from_np(a.dtype), kind="ExternalInput").ap()

    for name in _INS:
        given(name, np.ascontiguousarray(inputs[name]))
    given("consts", constants())
    out = nc.dram_tensor("out_0_dram", (1, S, D), F32, kind="ExternalOutput").ap()
    decoder_kernel(nc, aps["x"], aps["positions"], aps["consts"], aps, out)
    r = _run(nc, [arrays], core_ids=[0])
    return r.results[0]["out_0_dram"]
```
